# Optimizing a Trainium2 kernel written in Bass

```python
import jax
import jax.numpy as jnp
from jax import lax
import numpy as np

D_MODEL = 1024
BATCH = 1
SEQ = 256
DEPTH = 2
DEC_BATCH = 1
DEC_SEQ = 64
PAST_LEN = 256

CHUNK = 64
QBLOCK = 128
D_FF = 2816
FFN_RES_WEIGHT = 0.5
MLA_HEADS = 8
Q_LORA = 384
KV_LORA = 256
QK_NOPE = 64
QK_ROPE = 32
V_DIM = 64
MLA_WIDTH = MLA_HEADS * V_DIM
MLA_SCALE = (QK_NOPE + QK_ROPE) ** -0.5
ROPE_BASE = 10000.0
HG_HEADS = 4
HG_DK = 128
HG_DV = 128
HG_KWIDTH = HG_HEADS * HG_DK
HG_WIDTH = HG_HEADS * HG_DV
MIX_WIDTH = MLA_WIDTH + HG_WIDTH
IN_SPLITS = (Q_LORA, Q_LORA + KV_LORA, Q_LORA + KV_LORA + QK_ROPE,
             Q_LORA + KV_LORA + QK_ROPE + HG_KWIDTH,
             Q_LORA + KV_LORA + QK_ROPE + 2 * HG_KWIDTH,
             Q_LORA + KV_LORA + QK_ROPE + 2 * HG_KWIDTH + HG_WIDTH)
IN_COLS = Q_LORA + KV_LORA + QK_ROPE + 2 * HG_KWIDTH + 2 * HG_WIDTH
NORM_EPS = 1e-6
NEG_INF = -1e30

kernel_name = 'hymba_mla_hgrn2_macaron_stream'

def rmsnorm(x, g):
    xf = x.astype(jnp.float32)
    out = xf * lax.rsqrt(jnp.mean(xf * xf, axis=-1, keepdims=True) + NORM_EPS) * g.astype(jnp.float32)
    return out.astype(x.dtype)

def rope(x, pos):
    half = x.shape[-1] // 2
    inv = ROPE_BASE ** (-jnp.arange(half, dtype=jnp.float32) / half)
    ang = pos.astype(jnp.float32)[:, None] * inv
    ang = ang.reshape((x.shape[1],) + (1,) * (x.ndim - 3) + (half,))
    cos = jnp.cos(ang).astype(x.dtype)
    sin = jnp.sin(ang).astype(x.dtype)
    x1, x2 = x[..., :half], x[..., half:]
    return jnp.concatenate([x1 * cos - x2 * sin, x1 * sin + x2 * cos], axis=-1)

def swiglu(h, w_gu, w_down):
    gate, up = jnp.split(h @ w_gu, 2, axis=-1)
    return (jax.nn.silu(gate) * up) @ w_down

def mla_attention(q_nope, q_rope, lat, krope, w_ukv, offset):
    B, T, H, _ = q_nope.shape
    L = lat.shape[1]
    kv = (lat @ w_ukv).reshape(B, L, H, QK_NOPE + V_DIM)
    k_nope, v = kv[..., :QK_NOPE], kv[..., QK_NOPE:]
    outs = []
    for start in range(0, T, QBLOCK):
        stop = min(start + QBLOCK, T)
        kend = min(L, offset + stop)
        s = (jnp.einsum('bqhd,bkhd->bhqk', q_nope[:, start:stop], k_nope[:, :kend])
             + jnp.einsum('bqhr,bkr->bhqk', q_rope[:, start:stop], krope[:, :kend]))
        s = s.astype(jnp.float32) * MLA_SCALE
        q_chunk = (offset + jnp.arange(start, stop)) // CHUNK
        k_chunk = jnp.arange(kend) // CHUNK
        mask = k_chunk[None, :] <= q_chunk[:, None]
        p = jax.nn.softmax(jnp.where(mask, s, NEG_INF), axis=-1).astype(v.dtype)
        outs.append(jnp.einsum('bhqk,bkhd->bqhd', p, v[:, :kend]))
    return jnp.concatenate(outs, axis=1).reshape(B, T, H * V_DIM)

def hgrn2_chunked(q, k, log_f, v, s0):
    B, T, H, DK = q.shape
    DV = v.shape[-1]
    pad = (-T) % CHUNK
    if pad:
        padw = ((0, 0), (0, pad), (0, 0), (0, 0))
        q, k, log_f, v = [jnp.pad(a, padw) for a in (q, k, log_f, v)]
    NC = (T + pad) // CHUNK

    def to_chunks(a):
        return jnp.moveaxis(a.reshape(B, NC, CHUNK, H, a.shape[-1]), 2, 0)

    qc, kc, fc, vc = to_chunks(q), to_chunks(k), to_chunks(log_f), to_chunks(v)

    def intra_step(s, inp):
        q_t, k_t, lf_t, v_t = inp
        s = s * jnp.exp(lf_t)[..., None] + k_t[..., None] * v_t[..., None, :]
        return s, jnp.einsum('bnhk,bnhkv->bnhv', q_t, s)

    s_loc, o_loc = lax.scan(intra_step, jnp.zeros((B, NC, H, DK, DV), q.dtype), (qc, kc, fc, vc))
    a = jnp.cumsum(fc, axis=0)

    def inter_step(s, inp):
        dec, sl = inp
        return s * dec[..., None] + sl, s

    s_final, s_in = lax.scan(inter_step, s0,
                             (jnp.moveaxis(jnp.exp(a[-1]), 1, 0), jnp.moveaxis(s_loc, 1, 0)))
    o_inter = jnp.einsum('cbnhk,nbhkv->cbnhv', qc * jnp.exp(a), s_in)
    o = jnp.moveaxis(o_loc + o_inter, 0, 2).reshape(B, NC * CHUNK, H, DV)[:, :T]
    return o, s_final

def token_mixer(h, pos, lat_past, krope_past, s0, lb, p):
    B, T, _ = h.shape
    cq, ckv, kr, hq, hf, hi, hg = jnp.split(h @ p['w_in'], IN_SPLITS, axis=-1)
    q = (rmsnorm(cq, p['q_norm_gain']) @ p['w_uq']).reshape(B, T, MLA_HEADS, QK_NOPE + QK_ROPE)
    q_nope, q_rope = q[..., :QK_NOPE], rope(q[..., QK_NOPE:], pos)
    ckv = rmsnorm(ckv, p['kv_norm_gain'])
    krope = rope(kr, pos)
    if lat_past is None:
        keys_lat, keys_rope, offset = ckv, krope, 0
    else:
        keys_lat = jnp.concatenate([lat_past, ckv], axis=1)
        keys_rope = jnp.concatenate([krope_past, krope], axis=1)
        offset = lat_past.shape[1]
    attn = rmsnorm(mla_attention(q_nope, q_rope, keys_lat, keys_rope, p['w_ukv'], offset), p['mla_out_gain'])
    z = hf.astype(jnp.float32)
    log_f = jnp.logaddexp(jnp.log(lb), jnp.log1p(-lb) + jax.nn.log_sigmoid(z))
    k = (1.0 - lb) * jax.nn.sigmoid(-z)
    o, s_final = hgrn2_chunked(hq.astype(jnp.float32).reshape(B, T, HG_HEADS, HG_DK),
                               k.reshape(B, T, HG_HEADS, HG_DK),
                               log_f.reshape(B, T, HG_HEADS, HG_DK),
                               hi.astype(jnp.float32).reshape(B, T, HG_HEADS, HG_DV),
                               s0.astype(jnp.float32))
    o = rmsnorm(o, p['hg_norm_gain']) * jax.nn.silu(hg.astype(jnp.float32).reshape(B, T, HG_HEADS, HG_DV))
    o = o.reshape(B, T, HG_WIDTH).astype(h.dtype)
    y = jnp.concatenate([attn, o], axis=-1) @ p['w_out']
    return y, ckv, krope, s_final.astype(h.dtype)

def layer_forward(x, pos, lat_past, krope_past, s0, lb, p):
    g = p['norm_gains']
    x = x + FFN_RES_WEIGHT * rmsnorm(swiglu(rmsnorm(x, g[0]), p['ffa_w_gu'], p['ffa_w_down']), g[1])
    y, ckv, krope, s_final = token_mixer(rmsnorm(x, g[2]), pos, lat_past, krope_past, s0, lb, p)
    x = x + rmsnorm(y, g[3])
    x = x + FFN_RES_WEIGHT * rmsnorm(swiglu(rmsnorm(x, g[4]), p['ffb_w_gu'], p['ffb_w_down']), g[5])
    return x, ckv, krope, s_final

def setup_inputs(seed: int = 0) -> dict:
    key = jax.random.key(seed)
    ks = jax.random.split(key, 19)

    def nrm(k, shape, scale):
        return jax.random.normal(k, shape, jnp.float32) * scale

    def gain(k, shape):
        return 1.0 + 0.05 * jax.random.normal(k, shape, jnp.float32)

    return {
        'x_prompt': nrm(ks[0], (BATCH, SEQ, D_MODEL), 1.0),
        'x_sample': nrm(ks[1], (DEC_BATCH, DEC_SEQ, D_MODEL), 1.0),
        'cache_mla_latent': nrm(ks[2], (DEPTH, DEC_BATCH, PAST_LEN, KV_LORA), 1.0),
        'cache_mla_krope': nrm(ks[3], (DEPTH, DEC_BATCH, PAST_LEN, QK_ROPE), 1.0),
        'state_hgrn': nrm(ks[4], (DEPTH, DEC_BATCH, HG_HEADS, HG_DK, HG_DV), 0.3),
        'norm_gains': gain(ks[5], (DEPTH, 6, D_MODEL)),
        'ffa_w_gu': nrm(ks[6], (DEPTH, D_MODEL, 2 * D_FF), D_MODEL ** -0.5),
        'ffa_w_down': nrm(ks[7], (DEPTH, D_FF, D_MODEL), D_FF ** -0.5),
        'ffb_w_gu': nrm(ks[8], (DEPTH, D_MODEL, 2 * D_FF), D_MODEL ** -0.5),
        'ffb_w_down': nrm(ks[9], (DEPTH, D_FF, D_MODEL), D_FF ** -0.5),
        'w_in': nrm(ks[10], (DEPTH, D_MODEL, IN_COLS), D_MODEL ** -0.5),
        'q_norm_gain': gain(ks[11], (DEPTH, Q_LORA)),
        'w_uq': nrm(ks[12], (DEPTH, Q_LORA, MLA_HEADS * (QK_NOPE + QK_ROPE)), Q_LORA ** -0.5),
        'kv_norm_gain': gain(ks[13], (DEPTH, KV_LORA)),
        'w_ukv': nrm(ks[14], (DEPTH, KV_LORA, MLA_HEADS * (QK_NOPE + V_DIM)), KV_LORA ** -0.5),
        'mla_out_gain': gain(ks[15], (DEPTH, MLA_WIDTH)),
        'hg_lb_logits': nrm(ks[16], (DEPTH, HG_KWIDTH), 0.5),
        'hg_norm_gain': gain(ks[17], (DEPTH, HG_DV)),
        'w_out': nrm(ks[18], (DEPTH, MIX_WIDTH, D_MODEL), MIX_WIDTH ** -0.5),
    }

def reference(x_prompt, x_sample, cache_mla_latent, cache_mla_krope, state_hgrn,
              norm_gains, ffa_w_gu, ffa_w_down, ffb_w_gu, ffb_w_down, w_in,
              q_norm_gain, w_uq, kv_norm_gain, w_ukv, mla_out_gain,
              hg_lb_logits, hg_norm_gain, w_out):
    lbs = jnp.cumsum(jax.nn.softmax(hg_lb_logits.astype(jnp.float32), axis=0), axis=0)
    lbs = lbs - lbs[0:1]
    past_len = cache_mla_latent.shape[2]
    pos_p = jnp.arange(x_prompt.shape[1])
    pos_s = past_len + jnp.arange(x_sample.shape[1])
    s0_p = jnp.zeros((x_prompt.shape[0], HG_HEADS, HG_DK, HG_DV), x_prompt.dtype)
    h_p, h_s = x_prompt, x_sample
    lat_p, kr_p, st_p, lat_s, kr_s, st_s = [], [], [], [], [], []
    for l in range(DEPTH):
        p = {'norm_gains': norm_gains[l], 'ffa_w_gu': ffa_w_gu[l], 'ffa_w_down': ffa_w_down[l],
             'ffb_w_gu': ffb_w_gu[l], 'ffb_w_down': ffb_w_down[l], 'w_in': w_in[l],
             'q_norm_gain': q_norm_gain[l], 'w_uq': w_uq[l], 'kv_norm_gain': kv_norm_gain[l],
             'w_ukv': w_ukv[l], 'mla_out_gain': mla_out_gain[l], 'hg_norm_gain': hg_norm_gain[l],
             'w_out': w_out[l]}
        h_p, c, k, s = layer_forward(h_p, pos_p, None, None, s0_p, lbs[l], p)
        lat_p.append(c)
        kr_p.append(k)
        st_p.append(s)
        h_s, c, k, s = layer_forward(h_s, pos_s, cache_mla_latent[l], cache_mla_krope[l],
                                     state_hgrn[l], lbs[l], p)
        lat_s.append(c)
        kr_s.append(k)
        st_s.append(s)
    return (h_p, h_s, jnp.stack(lat_p), jnp.stack(kr_p), jnp.stack(st_p),
            jnp.stack(lat_s), jnp.stack(kr_s), jnp.stack(st_s))


_drawn_inputs = setup_inputs


def setup_inputs(seed=0):
    import zlib

    import numpy as np

    out = dict(_drawn_inputs(seed))
    spreads = {}
    factors = {}
    for name, (base, spread) in spreads.items():
        noise = np.random.default_rng([zlib.crc32(name.encode()), seed]).standard_normal(out[name].shape)
        drawn = base * np.exp(spread * noise) if base else spread * noise
        out[name] = jnp.asarray(drawn.astype(out[name].dtype))
    for name, factor in factors.items():
        out[name] = (out[name] * factor).astype(out[name].dtype)
    return out
```

```python
import concourse.bass as bass
from concourse import mybir
from contextlib import ExitStack

P = 128
D = 1024
DK = D // P
TP, TS = 256, 64
T = TP + TS
PAST = 256
KEYS = T + PAST
L = 2
FF = 2816
FT = FF // P
HALF = FT // 2
H = 8
NOPE, ROPE, VD = 64, 32, 64
QK = NOPE + ROPE
SCALE = QK ** -0.5
HG = 4
EPS = 1e-6
CQ, CKV = 3, 2

GU_A, DOWN_A, MIX, GU_B, DOWN_B = 0, FT, FT + 2 * DK, 58, 58 + FT
SLOTS = 2 * (FT + 2 * DK) + 20
SLOT = 2048
DOWN_W = HALF * P
S_IN, S_UQ, S_KN, S_V, S_IN2, S_OUT = 0, 6, 8, 9, 10, 16
MIX_SLOTS = 20
MIX_WIDTH = [SLOT] * 6 + [1536] * 2 + [1024] * 2 + [SLOT] * 5 + [1024] + [SLOT] * 4
M_CQ, M_CKV, M_KR, M_KRS, M_HF, M_HQ, M_HI, M_HG, M_END = 0, 3, 5, 6, 7, 11, 15, 19, 23
M_FIRST = 12

G_NORM, G_Q, G_KV, G_MLA, G_HG, G_LB, G_OML, G_END = 0, 48, 51, 53, 57, 58, 62, 66

QT = [(0, 128, 0, 128), (128, 128, 0, 256), (256, 64, 256, 320)]
GROUPS = [(0, range(0, 4)), (0, range(4, 8))] + [(1, range(h, h + 2)) for h in range(0, H, 2)] \
    + [(2, range(h, h + 1)) for h in range(H)]
NG = len(GROUPS)
LAST_GROUP = {1: 0, 5: 1, 13: 2}
VBLK = [(0, 128), (128, 128), (256, 64), (320, 128), (448, 128)]
KBLK = {0: [(0, 0)], 1: [(0, 0), (1, 128)], 2: [(2, 0), (3, 64), (4, 192)]}

HBLK = [(0, 128), (128, 128), (256, 64)]
LEVELS = [0, -1, 1, 2, 4, 8, 16, 32, 64]
NLEV = len(LEVELS)
FIRST_LEVEL_STEP = 3


FREE_AT_START = ("split_done", "slot_used", "gu_evac", "sg_ready", "a_ready", "a_lo_ready", "y_evac", "y_acc_ready")


def _jobs():
    jobs = []
    pre = [("m", m) for m in range(M_FIRST)] + [("uq", j) for j in range(8)] + [("kn", j) for j in range(8)] \
        + [("v", b) for b in range(5)]
    for n, job in enumerate(pre):
        act = job[0] == "v" or (job[0] == "kn" and job[1] % 2)
        jobs.append((job, n % 4, "act" if act else "dve"))
    steps = [("m", m) for m in range(M_FIRST, M_END)]
    for b in range(3):
        steps.insert(9 + 2 * b, ("vt", b))
    for n, job in enumerate(steps):
        jobs.append((job, n % 2, "act" if job[0] == "vt" else "dve"))
    tail = [("kt", b) for b in range(3)] + [("st", b) for b in range(3)] + [("o", h) for h in range(HG)] \
        + [("at", c) for c in range(4)] + [("hs", h) for h in range(HG)]
    for n, job in enumerate(tail):
        jobs.append((job, n % 4, "act" if job[0] in ("kt", "hs") else "dve"))
    return jobs


JOBS = _jobs()
NJ = len(JOBS)
JOB = {job: q for q, (job, _, _) in enumerate(JOBS)}
BANK = {job: bank for job, bank, _ in JOBS}
N_EVAC = {e: sum(x == e for _, _, x in JOBS) for e in ("dve", "act")}


def _emptied(job):
    q = JOB[job]
    e = JOBS[q][2]
    return e, sum(x == e for _, _, x in JOBS[:q + 1])


FFN_SLOTS = SLOTS - MIX_SLOTS


def _ffn_slot(n):
    return n if n < MIX else n - MIX_SLOTS


def _last_job(s):
    if s < S_UQ:
        return "m", 2 * s + 1
    if s < S_IN2:
        return [("uq", 3), ("uq", 7), ("kn", 7), ("v", 4)][s - S_UQ]
    return "m", min(M_FIRST + 2 * (s - S_IN2) + 1, M_END - 1)


def _before(job):
    q = JOB[job]
    same = [j for j, b, _ in JOBS[:q] if b == BANK[job]]
    return same[-1] if same else None


def trunk(nc, x_in, gains_in, cos_in, sin_in, ident_in, mask_in, wgu_in, wdn_in, wmix_in, latc_in, krc_in, s0_in,
          x_out, lat_out, kr_out, st_out):
    f32, f32r, u8 = mybir.dt.float32, mybir.dt.float32r, mybir.dt.uint8
    ALU, ACT, AX = mybir.AluOpType, mybir.ActivationFunctionType, mybir.AxisListType
    nbytes = {f32: 4, f32r: 4, u8: 1}

    top = [(nc.sbuf_base + 31) // 32 * 32]
    start = {}

    def at(name, shape, dt, offset):
        n = nbytes[dt]
        for d in shape[1:]:
            n *= d
        start[name] = (offset, (n + 31) // 32 * 32)
        return nc.alloc_sbuf_tensor_at(name, shape, dt, offset=offset)

    def new(name, shape, dt=f32):
        t = at(name, shape, dt, top[0])
        top[0] += start[name][1]
        return t

    def over(first, *tensors):
        out = []
        for name, shape, dt in tensors:
            out.append(at(name, shape, dt, first))
            first += start[name][1]
        return out, first

    x = new("x", [P, DK, T])
    h_hi, h_lo = new("h_hi", [P, DK, T], f32r), new("h_lo", [P, DK, T], f32r)
    raw = [new(f"raw{i}", [P, SLOT]) for i in range(2)]
    w_hi = [new(f"w_hi{i}", [P, SLOT], f32r) for i in range(2)]
    w_lo = [new(f"w_lo{i}", [P, SLOT], f32r) for i in range(2)]
    cos, sin = new("cos", [P, T]), new("sin", [P, T])
    ident, ones = new("ident", [P, P]), new("ones", [P, P])
    mask = new("mask", [P, NLEV, 64], u8)
    row_ind, neg = new("row_ind", [1, P]), new("neg", [1, 64])
    g_all, g = new("g_all", [P, L + 1, G_END]), new("g", [P, G_END])
    g_next = new("g_next", [P, DK])
    logit, e_logit = new("logit", [P, L, HG]), new("e_logit", [P, L, HG])
    lmax, lsum, cum = new("lmax", [P, HG]), new("lsum", [P, HG]), new("cum", [P, L, HG])
    y = new("y", [P, DK, T])
    scr = new("scr", [P, 8, T])
    rstd, yr, std = new("rstd", [P, T]), new("yr", [P, T]), new("std", [P, T])
    y_acc, x_acc = new("y_acc", [P, T]), new("x_acc", [P, T])
    lat = new("lat", [P, CKV, KEYS])
    c_sq, c_acc = new("c_sq", [P, 2, T]), new("c_acc", [P, 2, T])
    krr = new("krr", [P, T])
    mx, nmx, rs, rinv = (new(n, [P, 3, H]) for n in ("mx", "nmx", "rs", "rinv"))
    ss, sv, rn = (new(n, [P, 3]) for n in ("ss", "sv", "rn"))
    minus_half, eps = new("minus_half", [P, 3]), new("eps", [P, 1])
    o_junk = new("o_junk", [P, H * VD])
    c_std = new("c_std", [P, 2, T])
    r_q, r_kv = new("r_q", [P, T]), new("r_kv", [P, T])
    shared = top[0]
    (a_hi, a_lo), _ = over(shared, ("a_hi", [P, FT, T], f32r), ("a_lo", [P, FT, T], f32r))
    (q_h, k_h, v_tok, hq, hk, f_gate), end = over(
        shared, ("q_h", [QK, H, T], f32), ("k_h", [QK, H, KEYS], f32), ("v_tok", [P, 5, H * VD], f32),
        ("hq", [P, HG, T], f32), ("hk", [P, HG, T], f32), ("f_gate", [P, HG, T], f32))
    tots, end = over(end, *[(f"tot{1 << i}", [P, HG, T >> i], f32) for i in range(1, 7)],
                     ("tot128", [P, HG, 2], f32))
    tot = {1: f_gate, **{1 << i: t for i, t in enumerate(tots, 1)}}
    cq_at = end
    (cq_hi, cq_lo), end = over(cq_at, ("cq_hi", [P, CQ, T], f32r), ("cq_lo", [P, CQ, T], f32r))
    (tri_p, tri_s, s0), _ = over(cq_at, ("tri_p", [P, 2 * HG, P], f32), ("tri_s", [64, HG, 64], f32),
                                 ("s0", [P, HG, P], f32))
    lat_at = end
    (lat_hi, lat_lo, cos_r, sin_r), end = over(lat_at, ("lat_hi", [P, CKV, KEYS], f32r),
                                               ("lat_lo", [P, CKV, KEYS], f32r),
                                               ("cos_r", [P, T], f32), ("sin_r", [P, T], f32))
    (pt, hv_tok), _ = over(lat_at, ("pt", [P, 2, 512], f32), ("hv_tok", [P, 3, HG * P], f32))
    assert end <= nc.sbuf_usable_end
    (hk_tok, s1, s2, s_smp, o_hg), _ = over(start["k_h"][0], ("hk_tok", [P, 3, HG * P], f32), ("s1", [P, HG, P], f32),
                                            ("s2", [P, HG, P], f32), ("s_smp", [P, HG, P], f32),
                                            ("o_hg", [P, HG, T], f32))
    (o_sq, o_std), _ = over(start["q_h"][0], ("o_sq", [P, HG, T], f32), ("o_std", [P, HG, T], f32))
    (c32, kt1, kt2), _ = over(start["y"][0], ("c32", [P, CQ + CKV, T], f32), ("kt1", [P, T], f32),
                              ("kt2", [P, T], f32))
    (mask_raw,), _ = over(start["y"][0], ("mask_raw", [P, NLEV, 64], f32))
    (o_att, prob), _ = over(start["y"][0], ("o_att", [P, 3, H * VD], f32), ("prob", [P, 2, 512], f32))
    mix_hi, mix_lo = h_hi, h_lo

    ctx = ExitStack()
    with ctx:
        bank = [ctx.enter_context(nc.psum_tensor(f"bank{i}", [P, 512], f32)) for i in range(8)]
        sem = {}

        def S(name):
            if name not in sem:
                sem[name] = ctx.enter_context(nc.semaphore(name))
            return sem[name]

        for name in ("x_loaded const_loaded raw_ready0 raw_ready1 hi_ready split_done slot_used gs_ready "
                     "gu_evac sg_ready a_ready a_hi_ready a_lo_ready out_done y_evac y_acc_ready y_sum_done "
                     "y_std_ready yr_ready t_ready x_ready h_hi_ready h_ready x_sq_ready x_acc_ready x_sum_done "
                     "x_std_ready rstd_ready gains_ready gains_raw lb_step ones_ready job_done job_evac_dve "
                     "job_evac_act cs_krr krr_ready c_sq_ready c_acc_ready c_sum_done c_std_ready cr_ready "
                     "lat_ready cq_hi_ready cq_ready lat_hi_ready lat_lo_ready cs_q qt_ready sig_ready "
                     "gate_ready q_rope_ready k_rope_ready score_done max_ready nmax_ready exp_ready ptr_done "
                     "pt_ready pv_done rinv_ready o_evac o_ss_ready o_var_ready o_rn_ready o_att_ready "
                     "tri_zero level_done level_evac hq_up hk_up tot_up hg_silu o_sq_ready o_std_ready "
                     "o_r_ready o_t_ready o_g_ready mix_hi_ready mix_ready latc_ready krc_ready s0_ready side_out "
                     "state_out y_out lb_exp eps_ready mask_ready unread").split():
            S(name)
        block = ctx.enter_context(nc.Block())

        def nth(l, per_layer, n):
            return l * per_layer + n

        def wait_apart(eng, name, value):
            eng.wait_ge(S(name), value)
            eng.sem_inc(S("unread"), 1)

        def emptied(eng, l, job):
            e, n = _emptied(job)
            eng.wait_ge(S(f"job_evac_{e}"), nth(l, N_EVAC[e], n))

        def done(eng, l, job):
            eng.wait_ge(S("job_done"), nth(l, NJ, JOB[job] + 1))

        @block.sync
        def _(sp):
            sp.dma_start(x[:, 0:4, :], x_in[:, 0:4, :]).then_inc(S("x_loaded"), 16)
            sp.dma_start(g_all[:, 0:L, 0:G_LB], gains_in[:, :, 0:G_LB]).then_inc(S("gains_raw"), 16)
            sp.dma_start(logit[:, :, :], gains_in[:, :, G_LB:G_LB + HG]).then_inc(S("gains_raw"), 16)
            sp.dma_start(x[:, 4:8, :], x_in[:, 4:8, :]).then_inc(S("x_loaded"), 16)
            for name in FREE_AT_START:
                sp.sem_inc(S(name), 2)

            def load(l, n, par, dst, src):
                sp.wait_ge(S("split_done"), nth(l, SLOTS, n + 1))
                sp.dma_start(dst, src).then_inc(S(f"raw_ready{par}"), 16)

            def load_ffn(l, f, c0):
                with sp.Fori(0, FT // 2) as i:
                    for e in range(2):
                        load(l, i * 2 + (c0 + e), e, raw[e][:, :],
                             wgu_in[l * (2 * FT) + (i * 2 + (f * FT + e)), :, :])
                with sp.Fori(0, DK) as j:
                    for e in range(2):
                        load(l, j * 2 + (c0 + FT + e), e, raw[e][:, 0:DOWN_W],
                             wdn_in[l * (4 * DK) + (j * 2 + (f * 2 * DK + e)), :, :])

            with sp.Fori(0, L) as l:
                load_ffn(l, 0, GU_A)
                for s in range(MIX_SLOTS):
                    if s == 2:
                        sp.wait_ge(S("slot_used"), nth(l, FFN_SLOTS, MIX + 2))
                        for h in range(H):
                            sp.dma_start(k_h[NOPE:QK, h, T:KEYS], krc_in[l, :, :]).then_inc(S("krc_ready"), 16)
                        sp.dma_start(lat[:, :, T:KEYS], latc_in[l, :, :, :]).then_inc(S("latc_ready"), 16)
                    if s == S_IN2 + 1:
                        done(sp, l, ("uq", 7))
                        sp.dma_start(s0[:, :, :], s0_in[l, :, :, :]).then_inc(S("s0_ready"), 16)
                        sp.wait_ge(S("lat_ready"), nth(l, CKV, CKV))
                        sp.dma_start(lat_out[l, :, :, :], lat[:, :, 0:T]).then_inc(S("side_out"), 16)
                        sp.wait_ge(S("krr_ready"), nth(l, 1, 1))
                        sp.dma_start(kr_out[l, :, :], krr[0:ROPE, :]).then_inc(S("side_out"), 16)
                    if s == MIX_SLOTS - 1:
                        emptied(sp, l, ("st", 2))
                        sp.dma_start(st_out[l, 0, :, :, :], s2[:, :, :]).then_inc(S("state_out"), 16)
                        sp.dma_start(st_out[l, 1, :, :, :], s_smp[:, :, :]).then_inc(S("state_out"), 16)
                    w = MIX_WIDTH[s]
                    load(l, MIX + s, s % 2, raw[s % 2][:, 0:w], wmix_in[l * MIX_SLOTS + s, :, 0:w])
                load_ffn(l, 1, GU_B)
            load(0, L * SLOTS, 0, raw[0][:, 0:64], wgu_in[0, :, 0:64])
            for k in range(DK):
                sp.wait_ge(S("x_ready"), L * 3 * DK - DK + k + 1)
                sp.dma_start(x_out[:, k, :], x[:, k, :]).then_inc(S("y_out"), 16)
            sp.wait_ge(S("y_out"), 16 * DK)
            sp.wait_ge(S("side_out"), 32 * L)
            sp.wait_ge(S("state_out"), 32 * L)

        @block.tensor
        def _(pe):
            def split3(out, w, blk, m_w, rhs_hi, rhs_lo, first, last):
                hi, lo = w_hi[w][:, blk:blk + m_w], w_lo[w][:, blk:blk + m_w]
                nc.tensor.matmul(out, hi, rhs_hi, start=first, stop=False)
                nc.tensor.matmul(out, hi, rhs_lo, start=False, stop=False)
                return nc.tensor.matmul(out, lo, rhs_hi, start=False, stop=last)

            def slot(l, n):
                pe.wait_ge(S("split_done"), nth(l, SLOTS, n + 3))

            def gu_tile(l, n, e, free, chunkwise):
                slot(l, n)
                pe.wait_ge(S("gu_evac"), free)
                for k in range(DK):
                    if chunkwise is not None:
                        pe.wait_ge(S("h_ready"), chunkwise + k + 1)
                    for gate_up in range(2):
                        last = split3(bank[2 * e + gate_up][:, 0:T], e, (2 * k + gate_up) * P, P, h_hi[:, k, :],
                                      h_lo[:, k, :], k == 0, k == DK - 1)
                last.then_inc(S("slot_used"), 1)

            def x_sum(l, group):
                pe.wait_ge(S("x_acc_ready"), nth(l, 3 * DK, DK * (group + 1)))
                nc.tensor.matmul(bank[7][:, 0:T], ones[:, :], x_acc[:, :], start=True, stop=True)\
                    .then_inc(S("x_sum_done"), 1)

            def gate_up_phase(l, f, c0):
                tb = f * FT
                group = 2 * f
                gu_tile(l, c0, 0, nth(l, 2 * FT, tb + 1), nth(l, 3 * DK, DK * group))
                x_sum(l, group)
                gu_tile(l, c0 + 1, 1, nth(l, 2 * FT, tb + 2), None)
                with pe.Fori(1, FT // 2) as i:
                    for e in range(2):
                        gu_tile(l, i * 2 + (c0 + e), e, l * (2 * FT) + (i * 2 + (tb + e + 1)), None)

            def down_chunk(l, f, c, e, free, chunkwise):
                out = bank[4 + e][:, 0:T]
                for s in range(2):
                    slot(l, c + s)
                    if s == 0:
                        pe.wait_ge(S("y_evac"), free)
                    for kk in range(HALF):
                        k = s * HALF + kk
                        if chunkwise:
                            pe.wait_ge(S("a_lo_ready"), nth(l, 2 * FT, f * FT + k + 3))
                        last = split3(out, s, kk * P, P, a_hi[:, k, :], a_lo[:, k, :], k == 0, k == FT - 1)
                    last.then_inc(S("slot_used"), 1)

            def y_sum(l, b):
                pe.wait_ge(S("y_acc_ready"), nth(l, 3 * DK, DK * (b + 1) + 2))
                nc.tensor.matmul(bank[7][:, 0:T], ones[:, :], y_acc[:, :], start=True, stop=True)\
                    .then_inc(S("y_sum_done"), 1)

            def down_phase(l, f, c0):
                b = 2 * f
                down_chunk(l, f, c0, 0, nth(l, 3 * DK, b * DK + 1), True)
                with pe.Fori(0, 3) as i:
                    for e in range(2):
                        down_chunk(l, f, i * 4 + (c0 + 2 + 2 * e), 1 - e, l * (3 * DK) + (i * 2 + (b * DK + 2 + e)),
                                   False)
                down_chunk(l, f, c0 + 14, 1, nth(l, 3 * DK, b * DK + 8), False)
                y_sum(l, b)

            def begin(l, job):
                if _before(job) is not None:
                    emptied(pe, l, _before(job))
                return bank[BANK[job]]

            def m_tile(l, m, n, e):
                out = begin(l, ("m", m))[:, 0:T]
                if e == 0:
                    slot(l, MIX + n)
                for k in range(DK):
                    if m == 0:
                        pe.wait_ge(S("h_ready"), nth(l, 3 * DK, DK + k + 1))
                    last = split3(out, n % 2, (e * DK + k) * P, P, h_hi[:, k, :], h_lo[:, k, :], k == 0, k == DK - 1)
                last.then_inc(S("job_done"), 1)

            def scores(l, n):
                qt, heads = GROUPS[n]
                q0, nq, k0, nk = QT[qt]
                if n >= 2:
                    pe.wait_ge(S("exp_ready"), nth(l, NG, n - 1))
                for i, h in enumerate(heads):
                    out = bank[2 + n % 2][0:nq, i * nk:(i + 1) * nk]
                    last = nc.tensor.matmul(out, q_h[:, h, q0:q0 + nq], k_h[:, h, k0:k0 + nk], start=True,
                                            stop=qt == 2)
                    if qt < 2:
                        last = nc.tensor.matmul(out[:, nk - 64:nk], row_ind[:, :], neg[:, :], start=False, stop=True)
                last.then_inc(S("score_done"), 1)

            def prob_transposes(l, n):
                qt, heads = GROUPS[n]
                q0, nq, k0, nk = QT[qt]
                if n >= 1:
                    pe.wait_ge(S("pt_ready"), nth(l, NG, n))
                wait_apart(pe, "exp_ready", nth(l, NG, n + 1))
                c = 0
                for i, h in enumerate(heads):
                    for b, off in KBLK[qt]:
                        kb = VBLK[b][1]
                        last = nc.tensor.transpose(bank[4][0:kb, c:c + nq],
                                                   prob[0:nq, n % 2, i * nk + off:i * nk + off + kb],
                                                   ident[0:nq, 0:nq])
                        c += nq
                last.then_inc(S("ptr_done"), 1)

            def values(l, n):
                qt, heads = GROUPS[n]
                q0, nq, k0, nk = QT[qt]
                if n in (2, 6):
                    pe.wait_ge(S("o_evac"), nth(l, 3, qt))
                wait_apart(pe, "pt_ready", nth(l, NG, n + 1))
                c = 0
                for h in heads:
                    for b, off in KBLK[qt]:
                        kb = VBLK[b][1]
                        last = nc.tensor.matmul(bank[5][0:nq, h * VD:(h + 1) * VD], pt[0:kb, n % 2, c:c + nq],
                                                v_tok[0:kb, b, h * VD:(h + 1) * VD], start=off == 0,
                                                stop=b == KBLK[qt][-1][0])
                        c += nq
                last.then_inc(S("pv_done"), 1)

            def level(l, v):
                half = LEVELS[v]
                if v == 0:
                    emptied(pe, l, ("m", M_HQ + 3))
                    pe.wait_ge(S("gate_ready"), nth(l, HG, HG))
                else:
                    pe.wait_ge(S("level_evac"), nth(l, NLEV, v))
                if v >= 2:
                    pe.wait_ge(S("hq_up"), nth(l, NLEV - 1, v - 1))
                if v >= 3:
                    pe.wait_ge(S("hk_up"), nth(l, NLEV - 2, v - 2))
                for b, (t0, nt) in enumerate(HBLK):
                    if half == 64 and b == 2:
                        continue
                    for h in range(HG):
                        q = hq[:, h, t0:t0 + nt]
                        if half <= 0:
                            q = q.rearrange("p (n two) -> p two n", two=2)[:, -half, :]
                        else:
                            q = q.rearrange("p (n two s) -> p two n s", two=2, s=half)[:, 1, :, :]
                        if b < 2:
                            out = bank[6][:, (b * HG + h) * 64:(b * HG + h + 1) * 64]
                        else:
                            out = bank[7][0:64, h * 32:(h + 1) * 32]
                        last = nc.tensor.matmul(out, hk[:, h, t0:t0 + nt], q, start=True, stop=True)
                last.then_inc(S("level_done"), 1)

            def head_transposes(l, job, src):
                t0, nt = HBLK[job[1]]
                e, n = _emptied(_before(job))
                wait_apart(pe, f"job_evac_{e}", nth(l, N_EVAC[e], n))
                out = bank[BANK[job]]
                for h in range(HG):
                    last = nc.tensor.transpose(out[0:nt, h * P:(h + 1) * P], src[:, h, t0:t0 + nt], ident[:, :])
                last.then_inc(S("job_done"), 1)

            def mixer(l):
                for n in range(S_UQ):
                    for e in range(2):
                        m = 2 * n + e
                        m_tile(l, m, n, e)
                        if m == 1:
                            x_sum(l, 1)
                        if m == M_KR:
                            pe.wait_ge(S("c_acc_ready"), nth(l, 5, 3))
                            nc.tensor.matmul(bank[6][:, 0:T], ones[:, :], c_acc[:, 0, :], start=True, stop=True)\
                                .then_inc(S("c_sum_done"), 1)
                        if m == M_HF:
                            pe.wait_ge(S("c_acc_ready"), nth(l, 5, 5))
                            nc.tensor.matmul(bank[5][:, 0:T], ones[:, :], c_acc[:, 1, :], start=True, stop=True)\
                                .then_inc(S("c_sum_done"), 1)
                for j in range(8):
                    out = begin(l, ("uq", j))[:, 0:T]
                    w = (S_UQ + j // 4) % 2
                    if j % 4 == 0:
                        slot(l, MIX + S_UQ + j // 4)
                    if j == 0:
                        pe.wait_ge(S("cq_ready"), nth(l, CQ, CQ))
                    for k in range(CQ):
                        last = split3(out, w, ((j % 4) * CQ + k) * P, P, cq_hi[:, k, :], cq_lo[:, k, :], k == 0,
                                      k == CQ - 1)
                    last.then_inc(S("job_done"), 1)
                slot(l, MIX + S_KN)
                pe.wait_ge(S("lat_lo_ready"), nth(l, 2, 2))
                for j in range(8):
                    out = begin(l, ("kn", j))[:, 0:KEYS // 2]
                    cols = slice((j % 2) * KEYS // 2, (j % 2 + 1) * KEYS // 2)
                    for k in range(CKV):
                        last = split3(out, S_KN % 2, ((j // 2) * CKV + k) * P, P, lat_hi[:, k, cols],
                                      lat_lo[:, k, cols], k == 0, k == CKV - 1)
                    last.then_inc(S("job_done"), 1)
                slot(l, MIX + S_V)
                for b, (k0, kb) in enumerate(VBLK):
                    out = begin(l, ("v", b))[0:kb, :]
                    for k in range(CKV):
                        hi, lo = (t[:, k, k0:k0 + kb] for t in (lat_hi, lat_lo))
                        w_h, w_l = (t[S_V % 2][:, k * 512:(k + 1) * 512] for t in (w_hi, w_lo))
                        nc.tensor.matmul(out, hi, w_h, start=k == 0, stop=False)
                        nc.tensor.matmul(out, hi, w_l, start=False, stop=False)
                        last = nc.tensor.matmul(out, lo, w_h, start=False, stop=k == CKV - 1)
                    last.then_inc(S("job_done"), 1)
                emptied(pe, l, ("v", 2))
                emptied(pe, l, ("v", 3))
                emptied(pe, l, ("kn", 6))
                pe.wait_ge(S("q_rope_ready"), nth(l, 1, 1))
                pe.wait_ge(S("k_rope_ready"), nth(l, 1, 1))
                pe.wait_ge(S("krc_ready"), nth(l, 16 * H, 16 * H))
                for s in range(NG + 2):
                    if s < NG:
                        scores(l, s)
                    m = M_FIRST + s
                    if m < M_END:
                        m_tile(l, m, S_IN2 + s // 2, s % 2)
                    if 1 <= s <= NG:
                        prob_transposes(l, s - 1)
                    if s >= 2:
                        values(l, s - 2)
                    if 0 <= s - FIRST_LEVEL_STEP < NLEV:
                        level(l, s - FIRST_LEVEL_STEP)
                    if 8 <= s <= 10:
                        if s == 8:
                            emptied(pe, l, ("m", M_HI + 3))
                        head_transposes(l, ("vt", s - 8), scr)
                pe.wait_ge(S("hk_up"), nth(l, NLEV - 2, NLEV - 2))
                for b in range(3):
                    head_transposes(l, ("kt", b), hk)
                for b, (t0, nt) in enumerate(HBLK):
                    out = begin(l, ("st", b))
                    emptied(pe, l, ("kt", b))
                    emptied(pe, l, ("vt", b))
                    for h in range(HG):
                        cols = slice(h * P, (h + 1) * P)
                        last = nc.tensor.matmul(out[:, cols], hk_tok[0:nt, b, cols], hv_tok[0:nt, b, cols],
                                                start=True, stop=True)
                    last.then_inc(S("job_done"), 1)
                pe.wait_ge(S("level_evac"), nth(l, NLEV, NLEV))
                pe.wait_ge(S("hq_up"), nth(l, NLEV - 1, NLEV - 1))
                pe.wait_ge(S("s0_ready"), nth(l, 16, 16))
                emptied(pe, l, ("st", 0))
                for h in range(HG):
                    out = begin(l, ("o", h))
                    cols = slice(h * P, (h + 1) * P)
                    nc.tensor.matmul(out[:, 0:128], hv_tok[:, 0, cols], tri_p[:, h, :], start=True, stop=True)
                    nc.tensor.matmul(out[:, 128:256], hv_tok[:, 1, cols], tri_p[:, HG + h, :], start=True, stop=False)
                    nc.tensor.matmul(out[:, 128:256], s1[:, h, :], hq[:, h, 128:256], start=False, stop=True)
                    nc.tensor.matmul(out[:, 256:320], hv_tok[0:64, 2, cols], tri_s[:, h, :], start=True, stop=False)
                    nc.tensor.matmul(out[:, 256:320], s0[:, h, :], hq[:, h, 256:320], start=False, stop=True)\
                        .then_inc(S("job_done"), 1)
                pe.wait_ge(S("o_att_ready"), nth(l, 3, 3))
                for c in range(4):
                    out = begin(l, ("at", c))
                    for q0, nq, _, _ in QT:
                        qt = q0 // P
                        last = nc.tensor.transpose(out[:, q0:q0 + nq], o_att[0:nq, qt, c * P:(c + 1) * P],
                                                   ident[0:nq, 0:nq])
                    last.then_inc(S("job_done"), 1)
                for h in range(HG):
                    out = begin(l, ("hs", h))
                    pe.wait_ge(S("o_sq_ready"), nth(l, HG, h + 1))
                    nc.tensor.matmul(out[:, 0:T], ones[:, :], o_sq[:, h, :], start=True, stop=True)\
                        .then_inc(S("job_done"), 1)
                for j in range(DK):
                    n = S_OUT + j // 2
                    if j % 2 == 0:
                        slot(l, MIX + n)
                    pe.wait_ge(S("y_evac"), nth(l, 3 * DK, DK + j + 1))
                    for k in range(DK):
                        if j == 0:
                            if k < 4:
                                emptied(pe, l, ("at", k))
                            else:
                                pe.wait_ge(S("mix_ready"), nth(l, HG, k - 3))
                        last = split3(bank[4 + j % 2][:, 0:T], n % 2, ((j % 2) * DK + k) * P, P, mix_hi[:, k, :],
                                      mix_lo[:, k, :], k == 0, k == DK - 1)
                    last.then_inc(S("out_done"), 1)
                y_sum(l, 1)

            pe.wait_ge(S("ones_ready"), 2)
            pe.wait_ge(S("const_loaded"), 16 * 4)
            with pe.Fori(0, L) as l:
                gate_up_phase(l, 0, GU_A)
                down_phase(l, 0, DOWN_A)
                mixer(l)
                gate_up_phase(l, 1, GU_B)
                down_phase(l, 1, DOWN_B)

        @block.scalar
        def _(act):
            act.dma_start(cos[:, :], cos_in).then_inc(S("const_loaded"), 16)
            act.dma_start(sin[:, :], sin_in).then_inc(S("const_loaded"), 16)
            act.dma_start(ident[:, :], ident_in).then_inc(S("const_loaded"), 16)
            act.dma_start(mask_raw[:, :, :], mask_in).then_inc(S("const_loaded"), 16)

            def slot_free(l, n, mixer_slot):
                if mixer_slot is None:
                    act.wait_ge(S("slot_used"), nth(l, FFN_SLOTS, n + 1))
                elif mixer_slot < S_OUT:
                    done(act, l, _last_job(mixer_slot))
                else:
                    act.wait_ge(S("out_done"), nth(l, DK, 2 * (mixer_slot - S_OUT) + 2))

            def w_high(l, n, par, w, mixer_slot=None, after_mixer=0):
                act.wait_ge(S(f"raw_ready{par}"), nth(l, 8 * SLOTS, (n - par) * 8 + 16))
                slot_free(l, n - after_mixer if mixer_slot is None else n, mixer_slot)
                nc.scalar.activation(w_hi[par][:, 0:w], raw[par][:, 0:w], ACT.Copy).then_inc(S("hi_ready"), 1)

            def silu(t, e):
                act.wait_ge(S("gs_ready"), t + 1)
                act.wait_ge(S("a_ready"), t + 1)
                nc.scalar.activation(scr[:, 4 + e, :], scr[:, e, :], ACT.Silu).then_inc(S("sg_ready"), 1)

            def x_root(l, group):
                act.wait_ge(S("x_sum_done"), nth(l, 3, group + 1))
                nc.scalar.activation(std[:, :], bank[7][:, 0:T], ACT.Sqrt, bias=eps[:, 0:1], scale=1.0 / D)\
                    .then_inc(S("x_std_ready"), 1)

            def norm_chunk(before, k, gain):
                nc.scalar.activation(h_hi[:, k, :], x[:, k, :], ACT.Copy, scale=gain).then_inc(S("h_hi_ready"), 1)
                if k >= 6:
                    act.wait_ge(S("x_acc_ready"), before + (k - 5))
                nc.scalar.activation(scr[:, 2 + k % 6, :], x[:, k, :], ACT.Square).then_inc(S("x_sq_ready"), 1)

            def evac_chunk(j, e, dst, ended, count):
                act.wait_ge(S("y_acc_ready"), j + 1)
                act.wait_ge(S(ended), count)
                nc.scalar.activation(scr[:, e, :], bank[4 + e][:, 0:T], ACT.Square)
                nc.scalar.activation(dst, bank[4 + e][:, 0:T], ACT.Copy).then_inc(S("y_evac"), 1)

            def boundary(l, b, gain):
                ended = ("out_done", nth(l, DK, DK)) if b == 1 else \
                    ("slot_used", nth(l, FFN_SLOTS, _ffn_slot((DOWN_A, None, DOWN_B)[b]) + 18))
                evac_chunk(nth(l, 3 * DK, b * DK + 7), 1, y[:, 7, :], *ended)
                act.wait_ge(S("y_sum_done"), nth(l, 3, b + 1))
                nc.scalar.activation(std[:, :], bank[7][:, 0:T], ACT.Sqrt, bias=eps[:, 0:1], scale=1.0 / D)\
                    .then_inc(S("y_std_ready"), 1)
                for k in range(DK):
                    act.wait_ge(S("x_ready"), nth(l, 3 * DK, b * DK + k + 1))
                    norm_chunk(nth(l, 3 * DK, DK * (b + 1)), k, gain[:, k:k + 1])

            def gate_up_phase(l, f, c0):
                tb = f * FT
                am = MIX_SLOTS * f
                w_high(l, c0 + 1, 1, SLOT, MIX_SLOTS - 1 if f else None, am)
                x_root(l, 2 * f)
                w_high(l, c0 + 2, 0, SLOT, None, am)
                silu(nth(l, 2 * FT, tb), 0)
                with act.Fori(1, HALF) as i:
                    for e in range(2):
                        w_high(l, i * 2 + (c0 + e + 1), 1 - e, SLOT, None, am)
                        silu(l * (2 * FT) + (i * 2 + (tb + e - 1)), 1 - e)

            def down_phase(l, f, c0, after):
                b, am = 2 * f, MIX_SLOTS * f
                w_high(l, c0 + 1, 1, DOWN_W, None, am)
                silu(nth(l, 2 * FT, f * FT + FT - 1), 1)
                w_high(l, c0 + 2, 0, DOWN_W, None, am)
                with act.Fori(0, 3) as i:
                    for e in range(2):
                        w_high(l, i * 4 + (c0 + 3 + 2 * e), 1, DOWN_W, None, am)
                        evac_chunk(l * (3 * DK) + (i * 2 + (b * DK + e)), e, y[:, bass.ds(i * 2 + e, 1), :],
                                   "slot_used", l * FFN_SLOTS + (i * 4 + (_ffn_slot(c0) + 2 * e + 4)))
                        w_high(l, i * 4 + (c0 + 4 + 2 * e), 0, DOWN_W, None, am)
                w_high(l, c0 + 15, 1, DOWN_W, None, am)
                evac_chunk(nth(l, 3 * DK, b * DK + 6), 0, y[:, 6, :], "slot_used",
                           nth(l, FFN_SLOTS, _ffn_slot(c0) + 16))
                w_high(l, c0 + 16, 0, after, None, am)

            def mix_high(l, s):
                n = s + 1
                w_high(l, MIX + n, n % 2, MIX_WIDTH[n] if n < MIX_SLOTS else SLOT, n - 2 if n >= 2 else None)

            def c_square(l, j):
                act.wait_ge(S("job_evac_dve"), nth(l, N_EVAC["dve"], _emptied(("m", j))[1]))
                if j >= 2:
                    act.wait_ge(S("c_acc_ready"), nth(l, 5, j - 1))
                nc.scalar.activation(c_sq[:, j % 2, :], c32[:, j, :], ACT.Square).then_inc(S("c_sq_ready"), 1)

            def c_root(l, i):
                act.wait_ge(S("c_sum_done"), nth(l, 2, i + 1))
                nc.scalar.activation(c_std[:, i, :], bank[6 - i][:, 0:T], ACT.Sqrt, bias=eps[:, 0:1],
                                     scale=1.0 / (P * (CKV if i else CQ))).then_inc(S("c_std_ready"), 1)

            def sigmoids(l, j):
                act.wait_ge(S("job_evac_dve"), nth(l, N_EVAC["dve"], _emptied(("m", M_HF + j))[1]))
                if j >= 1:
                    act.wait_ge(S("gate_ready"), nth(l, HG, j))
                nc.scalar.activation(scr[:, 6, :], scr[:, 4 + j % 2, :], ACT.Sigmoid)
                nc.scalar.activation(scr[:, 7, :], scr[:, 4 + j % 2, :], ACT.Sigmoid, scale=-1.0)\
                    .then_inc(S("sig_ready"), 1)

            def exps(l, n):
                qt, heads = GROUPS[n]
                q0, nq, k0, nk = QT[qt]
                act.wait_ge(S("nmax_ready"), nth(l, NG, n + 1))
                if n >= 2:
                    act.wait_ge(S("ptr_done"), nth(l, NG, n - 1))
                for i, h in enumerate(heads):
                    last = nc.scalar.activation(prob[0:nq, n % 2, i * nk:(i + 1) * nk],
                                                bank[2 + n % 2][0:nq, i * nk:(i + 1) * nk], ACT.Exp,
                                                bias=nmx[0:nq, qt, h:h + 1], scale=SCALE,
                                                accum_out=rs[0:nq, qt, h:h + 1])
                last.then_inc(S("exp_ready"), 1)

            def att_square(l, qt):
                nq = QT[qt][1]
                act.wait_ge(S("o_evac"), nth(l, 3, qt + 1))
                nc.scalar.activation(o_junk[0:nq, :], o_att[0:nq, qt, :], ACT.Square, accum_out=ss[0:nq, qt:qt + 1])\
                    .then_inc(S("o_ss_ready"), 1)

            def evac(l, job, dst, src):
                done(act, l, job)
                nc.scalar.activation(dst, src, ACT.Copy).then_inc(S("job_evac_act"), 1)

            def mixer(l):
                for n in range(S_UQ):
                    if n == 0:
                        mix_high(l, 0)
                        x_root(l, 1)
                    else:
                        mix_high(l, n)
                    if n in (1, 2):
                        c_square(l, 2 * n - 2)
                        c_square(l, 2 * n - 1)
                    if n == 3:
                        c_square(l, 4)
                        c_root(l, 0)
                        for k in range(CQ):
                            nc.scalar.activation(cq_hi[:, k, :], c32[:, k, :], ACT.Copy,
                                                 scale=g[:, G_Q + k:G_Q + k + 1]).then_inc(S("cq_hi_ready"), 1)
                    if n == 4:
                        c_root(l, 1)
                        sigmoids(l, 0)
                    if n == 5:
                        sigmoids(l, 1)
                        sigmoids(l, 2)
                act.wait_ge(S("latc_ready"), nth(l, 16, 16))
                nc.scalar.activation(lat_hi[:, :, T:KEYS], lat[:, :, T:KEYS], ACT.Copy).then_inc(S("lat_hi_ready"), 1)
                act.wait_ge(S("lat_ready"), nth(l, CKV, CKV))
                nc.scalar.activation(lat_hi[:, :, 0:T], lat[:, :, 0:T], ACT.Copy).then_inc(S("lat_hi_ready"), 1)
                sigmoids(l, 3)
                mix_high(l, S_UQ)
                mix_high(l, S_UQ + 1)
                mix_high(l, S_KN)
                for j in range(1, 8, 2):
                    job = ("kn", j)
                    src = bank[BANK[job]]
                    cols = slice(KEYS // 2, KEYS)
                    done(act, l, job)
                    nc.scalar.activation(k_h[0:NOPE, j - 1, cols], src[0:NOPE, 0:KEYS // 2], ACT.Copy)
                    nc.scalar.activation(k_h[0:NOPE, j, cols], src[NOPE:P, 0:KEYS // 2], ACT.Copy)\
                        .then_inc(S("job_evac_act"), 1)
                mix_high(l, S_V)
                for b, (k0, kb) in enumerate(VBLK):
                    evac(l, ("v", b), v_tok[0:kb, b, :], bank[BANK["v", b]][0:kb, :])
                for s in range(NG + 2):
                    if s % 2 == 0 and s <= 10:
                        mix_high(l, S_IN2 + s // 2)
                    if s < NG:
                        exps(l, s)
                    if s - 2 in LAST_GROUP:
                        att_square(l, LAST_GROUP[s - 2])
                    if 8 <= s <= 10:
                        b = s - 8
                        nt = HBLK[b][1]
                        evac(l, ("vt", b), hv_tok[0:nt, b, :], bank[BANK["vt", b]][0:nt, :])
                for b, (t0, nt) in enumerate(HBLK):
                    evac(l, ("kt", b), hk_tok[0:nt, b, :], bank[BANK["kt", b]][0:nt, :])
                act.wait_ge(S("job_evac_dve"), nth(l, N_EVAC["dve"], _emptied(("m", M_END - 1))[1]))
                nc.scalar.activation(scr[:, 4:8, :], scr[:, 4:8, :], ACT.Silu).then_inc(S("hg_silu"), 1)
                for h in range(HG):
                    act.wait_ge(S("job_evac_dve"), nth(l, N_EVAC["dve"], _emptied(("o", h))[1]))
                    nc.scalar.activation(o_sq[:, h, :], o_hg[:, h, :], ACT.Square).then_inc(S("o_sq_ready"), 1)
                for c in range(4):
                    done(act, l, ("at", c))
                    nc.scalar.activation(mix_hi[:, c, :], bank[BANK["at", c]][:, 0:T], ACT.Copy,
                                         scale=g[:, G_MLA + c:G_MLA + c + 1]).then_inc(S("mix_hi_ready"), 1)
                for h in range(HG):
                    job = ("hs", h)
                    done(act, l, job)
                    nc.scalar.activation(o_std[:, h, :], bank[BANK[job]][:, 0:T], ACT.Sqrt, bias=eps[:, 0:1],
                                         scale=1.0 / P).then_inc(S("job_evac_act"), 1)
                for h in range(HG):
                    act.wait_ge(S("o_g_ready"), nth(l, HG, h + 1))
                    nc.scalar.activation(mix_hi[:, 4 + h, :], o_hg[:, h, :], ACT.Copy).then_inc(S("mix_hi_ready"), 1)
                for j in range(DK):
                    if j % 2 == 0:
                        mix_high(l, S_OUT + j // 2)
                    if j < DK - 1:
                        evac_chunk(nth(l, 3 * DK, DK + j), j % 2, y[:, j, :], "out_done", nth(l, DK, j + 1))
                boundary(l, 1, g[:, G_NORM + 4 * DK:G_NORM + 5 * DK])

            act.wait_ge(S("gains_raw"), 32)
            act.wait_ge(S("eps_ready"), 1)
            act.wait_ge(S("x_loaded"), 32)
            for k in range(DK):
                norm_chunk(0, k, g_all[:, 0, k:k + 1])
            act.wait_ge(S("lb_step"), 2)
            nc.scalar.activation(e_logit[:, :, :], e_logit[:, :, :], ACT.Exp).then_inc(S("lb_exp"), 1)
            w_high(0, 0, 0, SLOT)
            with act.Fori(0, L) as l:
                gate_up_phase(l, 0, GU_A)
                down_phase(l, 0, DOWN_A, SLOT)
                boundary(l, 0, g[:, G_NORM + 2 * DK:G_NORM + 3 * DK])
                mixer(l)
                gate_up_phase(l, 1, GU_B)
                down_phase(l, 1, DOWN_B, SLOT)
                boundary(l, 2, g_next)

        @block.vector
        def _(dve):
            def w_low(l, n, par, w):
                dve.wait_ge(S("hi_ready"), nth(l, SLOTS, n + 1))
                nc.vector.tensor_tensor(w_lo[par][:, 0:w], raw[par][:, 0:w], w_hi[par][:, 0:w].bitcast(f32),
                                        ALU.subtract).then_inc(S("split_done"), 1)

            def hidden_evac(t, e, used):
                dve.wait_ge(S("slot_used"), used)
                dve.wait_ge(S("sg_ready"), t + 1)
                nc.vector.tensor_tensor(scr[:, e, :], bank[2 * e][:, 0:T], rstd[:, :], ALU.mult)\
                    .then_inc(S("gs_ready"), 1)
                dve.wait_ge(S("a_ready"), t + 1)
                nc.vector.tensor_tensor(scr[:, 2 + e, :], bank[2 * e + 1][:, 0:T], rstd[:, :], ALU.mult)\
                    .then_inc(S("gu_evac"), 1)

            def hidden_split(t, e, dst_hi, dst_lo):
                dve.wait_ge(S("a_ready"), t + 3)
                nc.vector.tensor_scalar(dst_hi, scr[:, 6 + e, :], 1.0, None, ALU.mult).then_inc(S("a_hi_ready"), 1)
                dve.wait_ge(S("a_hi_ready"), t + 1)
                nc.vector.tensor_tensor(dst_lo, scr[:, 6 + e, :], dst_hi.bitcast(f32), ALU.subtract)\
                    .then_inc(S("a_lo_ready"), 1)

            def x_factor(l, group):
                dve.wait_ge(S("x_std_ready"), nth(l, 3, group + 1))
                nc.vector.reciprocal(rstd[:, :], std[:, :]).then_inc(S("rstd_ready"), 1)
                dve.wait_ge(S("rstd_ready"), nth(l, 3, group + 1))

            def low_chunk(before, k, gain):
                dve.wait_ge(S("h_hi_ready"), before + (k + 1))
                nc.vector.scalar_tensor_tensor(h_lo[:, k, :], x[:, k, :], gain, h_hi[:, k, :].bitcast(f32), ALU.mult,
                                               ALU.subtract).then_inc(S("h_ready"), 1)

            def boundary(l, b, post, pre):
                dve.wait_ge(S("y_std_ready"), nth(l, 3, b + 1))
                nc.vector.reciprocal(yr[:, :], std[:, :]).then_inc(S("yr_ready"), 1)
                dve.wait_ge(S("yr_ready"), nth(l, 3, b + 1))
                if b == 0:
                    dve.wait_ge(S("gains_ready"), nth(l, 2, 2))
                for k in range(DK):
                    if k >= 2:
                        dve.wait_ge(S("x_ready"), nth(l, 3 * DK, b * DK + k - 1))
                    nc.vector.scalar_tensor_tensor(scr[:, k % 2, :], y[:, k, :], post[:, k:k + 1], yr[:, :],
                                                   ALU.mult, ALU.mult).then_inc(S("t_ready"), 1)
                    if k >= 1:
                        low_chunk(nth(l, 3 * DK, DK * (b + 1)), k - 1, pre[:, k - 1:k])
                low_chunk(nth(l, 3 * DK, DK * (b + 1)), DK - 1, pre[:, DK - 1:DK])

            def gate_up_phase(l, f, c0):
                tb = f * FT
                w_low(l, c0 + 1, 1, SLOT)
                x_factor(l, 2 * f)
                hidden_evac(nth(l, 2 * FT, tb), 0, nth(l, FFN_SLOTS, _ffn_slot(c0) + 3))
                w_low(l, c0 + 2, 0, SLOT)
                if f == 1:
                    dve.wait_ge(S("state_out"), nth(l, 32, 32))
                hidden_split(nth(l, 2 * FT, tb), 0, a_hi[:, 0, :], a_lo[:, 0, :])
                with dve.Fori(1, HALF) as i:
                    for e in range(2):
                        t = l * (2 * FT) + (i * 2 + (tb + e - 1))
                        hidden_evac(t, 1 - e, l * FFN_SLOTS + (i * 2 + (_ffn_slot(c0) + e + 2)))
                        w_low(l, i * 2 + (c0 + e + 1), 1 - e, SLOT)
                        at = bass.ds(i * 2 + (e - 1), 1)
                        hidden_split(t, 1 - e, a_hi[:, at, :], a_lo[:, at, :])

            def down_phase(l, f, c0, after):
                t = nth(l, 2 * FT, f * FT + FT - 1)
                hidden_evac(t, 1, nth(l, FFN_SLOTS, _ffn_slot(c0) + 2))
                w_low(l, c0 + 1, 1, DOWN_W)
                hidden_split(t, 1, a_hi[:, FT - 1, :], a_lo[:, FT - 1, :])
                w_low(l, c0 + 2, 0, DOWN_W)
                with dve.Fori(0, 6) as i:
                    w_low(l, i * 2 + (c0 + 3), 1, DOWN_W)
                    w_low(l, i * 2 + (c0 + 4), 0, DOWN_W)
                w_low(l, c0 + 15, 1, DOWN_W)
                w_low(l, c0 + 16, 0, after)

            def mix_low(l, s):
                n = s + 1
                w_low(l, MIX + n, n % 2, MIX_WIDTH[n] if n < MIX_SLOTS else SLOT)

            def m_evac(l, m):
                job = ("m", m)
                src = bank[BANK[job]][:, 0:T]
                if m in (M_KR, M_KRS):
                    dve.wait_ge(S("cs_krr"), nth(l, 1, 1))
                    dst, factor = (kt1, scr[:, 0, :]) if m == M_KR else (kt2, scr[:, 1, :])
                    dst = dst[:, :]
                else:
                    factor = rstd[:, :]
                    j = m - M_HF
                    if m < M_KR:
                        dst = c32[:, m, :]
                    elif m < M_HQ:
                        dst = scr[:, 4 + j % 2, :]
                        if j >= 2:
                            dve.wait_ge(S("sig_ready"), nth(l, HG, j - 1))
                    elif m < M_HI:
                        dst = hq[:, m - M_HQ, :]
                    else:
                        dst = scr[:, m - M_HI, :]
                done(dve, l, job)
                nc.vector.tensor_tensor(dst, src, factor, ALU.mult).then_inc(S("job_evac_dve"), 1)

            def gates(l, j):
                dve.wait_ge(S("sig_ready"), nth(l, HG, j + 1))
                nc.vector.tensor_scalar(f_gate[:, j, :], scr[:, 6, :], g[:, G_OML + j:G_OML + j + 1],
                                        g[:, G_LB + j:G_LB + j + 1], ALU.mult, ALU.add)
                nc.vector.tensor_scalar(hk[:, j, :], scr[:, 7, :], g[:, G_OML + j:G_OML + j + 1], None, ALU.mult)\
                    .then_inc(S("gate_ready"), 1)

            def group_max(l, n):
                qt, heads = GROUPS[n]
                q0, nq, k0, nk = QT[qt]
                hs = slice(heads[0], heads[-1] + 1)
                dve.wait_ge(S("score_done"), nth(l, NG, n + 1))
                nc.vector.tensor_reduce(mx[0:nq, qt, hs],
                                        bank[2 + n % 2][0:nq, 0:len(heads) * nk].rearrange("p (h k) -> p h k", k=nk),
                                        AX.X, ALU.max).then_inc(S("max_ready"), 1)
                dve.wait_ge(S("max_ready"), nth(l, NG, n + 1))
                nc.vector.tensor_scalar(nmx[0:nq, qt, hs], mx[0:nq, qt, hs], -SCALE, None, ALU.mult)\
                    .then_inc(S("nmax_ready"), 1)

            def pt_evac(l, n):
                qt, heads = GROUPS[n]
                dve.wait_ge(S("ptr_done"), nth(l, NG, n + 1))
                if n >= 2:
                    dve.wait_ge(S("pv_done"), nth(l, NG, n - 1))
                if qt < 2:
                    nc.vector.tensor_copy(pt[:, n % 2, :], bank[4][:, :]).then_inc(S("pt_ready"), 1)
                else:
                    nc.vector.tensor_copy(pt[0:64, n % 2, 0:64], bank[4][0:64, 0:64])
                    nc.vector.tensor_copy(pt[:, n % 2, 64:192], bank[4][:, 64:192]).then_inc(S("pt_ready"), 1)

            def o_evac(l, n):
                qt = LAST_GROUP[n]
                nq = QT[qt][1]
                dve.wait_ge(S("exp_ready"), nth(l, NG, n + 1))
                nc.vector.reciprocal(rinv[0:nq, qt, :], rs[0:nq, qt, :]).then_inc(S("rinv_ready"), 1)
                dve.wait_ge(S("rinv_ready"), nth(l, 3, qt + 1))
                dve.wait_ge(S("pv_done"), nth(l, NG, n + 1))
                nc.vector.tensor_tensor(o_att[0:nq, qt, :].rearrange("p (h d) -> p h d", d=VD),
                                        bank[5][0:nq, :].rearrange("p (h d) -> p h d", d=VD),
                                        rinv[0:nq, qt, :].unsqueeze(2).broadcast_to([nq, H, VD]), ALU.mult)\
                    .then_inc(S("o_evac"), 1)

            def o_var(l, qt):
                nq = QT[qt][1]
                dve.wait_ge(S("o_ss_ready"), nth(l, 3, qt + 1))
                nc.vector.tensor_scalar(sv[0:nq, qt:qt + 1], ss[0:nq, qt:qt + 1], 1.0 / (H * VD), EPS, ALU.mult,
                                        ALU.add).then_inc(S("o_var_ready"), 1)

            def o_scale(l, qt):
                nq = QT[qt][1]
                dve.wait_ge(S("o_rn_ready"), nth(l, 3, qt + 1))
                nc.vector.tensor_scalar(o_att[0:nq, qt, :], o_att[0:nq, qt, :], rn[0:nq, qt:qt + 1], None, ALU.mult)\
                    .then_inc(S("o_att_ready"), 1)

            def tri_view(t, half):
                if half <= 0:
                    return t.rearrange("p u (n two) -> p two u n", two=2)[:, -half, :, :]
                return t.rearrange("p u (n two s) -> p two u n s", two=2, s=half)[:, 1, :, :, :]

            def level_evac(l, v):
                half = LEVELS[v]
                wait_apart(dve, "level_done", nth(l, NLEV, v + 1))
                for t, src, nk, units, nq in ((tri_p[:, :, :], bank[6], P, 2 * HG, 64), (tri_s[:, :, :], bank[7], 64, HG, 32)):
                    if half == 64 and nq == 32:
                        continue
                    m = mask[0:nk, v, 0:nq]
                    d = src[0:nk, 0:units * nq]
                    if half <= 0:
                        m = m.unsqueeze(1).broadcast_to([nk, units, nq])
                        d = d.rearrange("p (u n) -> p u n", n=nq)
                    else:
                        m = m.rearrange("p (n s) -> p n s", s=half).unsqueeze(1)\
                            .broadcast_to([nk, units, nq // half, half])
                        d = d.rearrange("p (u n s) -> p u n s", n=nq // half, s=half)
                    last = nc.vector.copy_predicated(tri_view(t, half), m, d)
                last.then_inc(S("level_evac"), 1)

            def pairs(t, half):
                return t[:, :, :].rearrange("p h (n two s) -> p (h n) two s", two=2, s=half)

            def queries_up(l, v):
                dve.wait_ge(S("level_done"), nth(l, NLEV, v))
                if v == 2:
                    nc.vector.tensor_tensor(hq[:, :, :], hq[:, :, :], f_gate[:, :, :], ALU.mult)\
                        .then_inc(S("hq_up"), 1)
                    dve.wait_ge(S("hq_up"), nth(l, NLEV - 1, 1))
                    return
                half = LEVELS[v - 1]
                n_tot = v - 3
                dve.wait_ge(S("hq_up"), nth(l, NLEV - 1, v - 2))
                if n_tot:
                    dve.wait_ge(S("tot_up"), nth(l, NLEV - 2, n_tot))
                if half < 64:
                    q = pairs(hq, half)[:, :, 1, :]
                    two = tot[half][:, :, :].rearrange("p h (n two) -> p (h n) two", two=2)
                    first, second = two[:, :, 0], two[:, :, 1]
                    n = first.shape[1]
                    nc.vector.tensor_tensor(q, q, first.unsqueeze(2).broadcast_to([P, n, half]), ALU.mult)\
                        .then_inc(S("hq_up"), 1)
                    up = tot[2 * half][:, :, :].rearrange("p h n -> p (h n)")
                else:
                    q = hq[:, :, 0:TP].rearrange("p h (n two s) -> p h n two s", two=2, s=half)[:, :, :, 1, :]
                    two = tot[half][:, :, 0:4].rearrange("p h (n two) -> p h n two", two=2)
                    first, second = two[:, :, :, 0], two[:, :, :, 1]
                    nc.vector.tensor_tensor(q, q, first.unsqueeze(3).broadcast_to([P, HG, 2, half]), ALU.mult)\
                        .then_inc(S("hq_up"), 1)
                    up = tot[128][:, :, :]
                nc.vector.tensor_tensor(up, first, second, ALU.mult).then_inc(S("tot_up"), 1)

            def mixer(l):
                mix_low(l, 0)
                x_factor(l, 1)
                m_evac(l, 0)
                m_evac(l, 1)
                mix_low(l, 1)
                m_evac(l, 2)
                m_evac(l, 3)
                mix_low(l, 2)
                m_evac(l, 4)
                m_evac(l, M_KR)
                mix_low(l, 3)
                m_evac(l, M_KRS)
                dve.wait_ge(S("c_std_ready"), nth(l, 2, 1))
                nc.vector.reciprocal(r_q[:, :], c_std[:, 0, :]).then_inc(S("cr_ready"), 1)
                for k in range(CQ):
                    dve.wait_ge(S("cq_hi_ready"), nth(l, CQ, k + 1))
                    nc.vector.scalar_tensor_tensor(cq_lo[:, k, :], c32[:, k, :], g[:, G_Q + k:G_Q + k + 1],
                                                   cq_hi[:, k, :].bitcast(f32), ALU.mult, ALU.subtract)\
                        .then_inc(S("cq_ready"), 1)
                m_evac(l, M_HF)
                mix_low(l, 4)
                m_evac(l, M_HF + 1)
                dve.wait_ge(S("c_std_ready"), nth(l, 2, 2))
                nc.vector.reciprocal(r_kv[:, :], c_std[:, 1, :]).then_inc(S("cr_ready"), 1)
                dve.wait_ge(S("cr_ready"), nth(l, 2, 2))
                for k in range(CKV):
                    nc.vector.scalar_tensor_tensor(lat[:, k, 0:T], c32[:, CQ + k, :], g[:, G_KV + k:G_KV + k + 1],
                                                   r_kv[:, :], ALU.mult, ALU.mult).then_inc(S("lat_ready"), 1)
                gates(l, 0)
                m_evac(l, M_HF + 2)
                mix_low(l, 5)
                gates(l, 1)
                m_evac(l, M_HF + 3)
                gates(l, 2)
                m_evac(l, M_HQ)
                for i, cols in enumerate((slice(T, KEYS), slice(0, T))):
                    dve.wait_ge(S("lat_hi_ready"), nth(l, 2, i + 1))
                    nc.vector.tensor_tensor(lat_lo[:, :, cols], lat[:, :, cols], lat_hi[:, :, cols].bitcast(f32),
                                            ALU.subtract).then_inc(S("lat_lo_ready"), 1)
                gates(l, 3)
                mix_low(l, S_UQ)
                dve.wait_ge(S("krr_ready"), nth(l, 1, 1))
                nc.vector.tensor_copy(k_h[NOPE:QK, :, 0:T], krr[NOPE:QK, :].unsqueeze(1).broadcast_to([ROPE, H, T]))\
                    .then_inc(S("k_rope_ready"), 1)
                dve.wait_ge(S("cs_q"), nth(l, 1, 1))
                for j in range(8):
                    if j == 4:
                        mix_low(l, S_UQ + 1)
                    job = ("uq", j)
                    src = bank[BANK[job]]
                    done(dve, l, job)
                    if j < 4:
                        nc.vector.tensor_tensor(q_h[0:NOPE, 2 * j, :], src[0:NOPE, 0:T], r_q[0:NOPE, :], ALU.mult)
                        ins = nc.vector.tensor_tensor(q_h[0:NOPE, 2 * j + 1, :], src[NOPE:P, 0:T], r_q[NOPE:P, :],
                                                      ALU.mult)
                    else:
                        ins = nc.vector.tensor_tensor(scr[:, j - 4, :], src[:, 0:T],
                                                      (cos_r if j < 6 else sin_r)[:, :], ALU.mult)
                    ins.then_inc(S("job_evac_dve"), 1)
                dve.wait_ge(S("job_evac_dve"), nth(l, N_EVAC["dve"], _emptied(("uq", 7))[1]))
                for h in range(H):
                    rows = slice(h % 4 * ROPE, (h % 4 + 1) * ROPE)
                    ins = nc.vector.tensor_tensor(q_h[NOPE:QK, h, :], scr[rows, h // 4, :], scr[rows, 2 + h // 4, :],
                                                  ALU.add)
                ins.then_inc(S("q_rope_ready"), 1)
                nc.vector.memset(tri_p[:, :, :], 0.0)
                nc.vector.memset(tri_s[:, :, :], 0.0).then_inc(S("tri_zero"), 1)
                mix_low(l, S_KN)
                for j in range(0, 8, 2):
                    job = ("kn", j)
                    src = bank[BANK[job]]
                    done(dve, l, job)
                    nc.vector.tensor_copy(k_h[0:NOPE, j, 0:KEYS // 2], src[0:NOPE, 0:KEYS // 2])
                    nc.vector.tensor_copy(k_h[0:NOPE, j + 1, 0:KEYS // 2], src[NOPE:P, 0:KEYS // 2])\
                        .then_inc(S("job_evac_dve"), 1)
                mix_low(l, S_V)
                dve.wait_ge(S("tri_zero"), nth(l, 1, 1))
                for s in range(NG + 2):
                    if s < NG:
                        group_max(l, s)
                    if s % 2 == 0 and s <= 10:
                        mix_low(l, S_IN2 + s // 2)
                    if M_FIRST + s < M_END:
                        m_evac(l, M_FIRST + s)
                    if 1 <= s <= NG:
                        pt_evac(l, s - 1)
                    if s - 2 in LAST_GROUP:
                        o_evac(l, s - 2)
                        o_var(l, LAST_GROUP[s - 2])
                    if s - 3 in LAST_GROUP:
                        o_scale(l, LAST_GROUP[s - 3])
                    v = s - FIRST_LEVEL_STEP
                    if 0 <= v < NLEV:
                        level_evac(l, v)
                        if v >= 1:
                            queries_up(l, v + 1)
                for b in range(3):
                    job = ("st", b)
                    src = bank[BANK[job]]
                    done(dve, l, job)
                    if b == 0:
                        ins = nc.vector.tensor_copy(s1[:, :, :], src[:, :].rearrange("p (h d) -> p h d", h=HG))
                    else:
                        dve.wait_ge(S("tot_up"), nth(l, NLEV - 2, NLEV - 2))
                        if b == 1:
                            emptied(dve, l, ("st", 0))
                        else:
                            dve.wait_ge(S("s0_ready"), nth(l, 16, 16))
                        for h in range(HG):
                            before, after = (s1, s2) if b == 1 else (s0, s_smp)
                            decay = tot[128][:, h, 1:2] if b == 1 else tot[64][:, h, 4:5]
                            ins = nc.vector.scalar_tensor_tensor(after[:, h, :], before[:, h, :], decay,
                                                                 src[:, h * P:(h + 1) * P], ALU.mult, ALU.add)
                    ins.then_inc(S("job_evac_dve"), 1)
                for h in range(HG):
                    job = ("o", h)
                    done(dve, l, job)
                    nc.vector.tensor_copy(o_hg[:, h, :], bank[BANK[job]][:, 0:T]).then_inc(S("job_evac_dve"), 1)
                o_scale(l, 2)
                for c in range(4):
                    dve.wait_ge(S("mix_hi_ready"), nth(l, DK, c + 1))
                    nc.vector.scalar_tensor_tensor(mix_lo[:, c, :], bank[BANK["at", c]][:, 0:T],
                                                   g[:, G_MLA + c:G_MLA + c + 1], mix_hi[:, c, :].bitcast(f32),
                                                   ALU.mult, ALU.subtract).then_inc(S("job_evac_dve"), 1)
                for h in range(HG):
                    dve.wait_ge(S("job_evac_act"), nth(l, N_EVAC["act"], _emptied(("hs", h))[1]))
                    nc.vector.reciprocal(o_std[:, h, :], o_std[:, h, :]).then_inc(S("o_r_ready"), 1)
                    dve.wait_ge(S("o_r_ready"), nth(l, HG, h + 1))
                    nc.vector.scalar_tensor_tensor(o_hg[:, h, :], o_hg[:, h, :], g[:, G_HG:G_HG + 1], o_std[:, h, :],
                                                   ALU.mult, ALU.mult).then_inc(S("o_t_ready"), 1)
                for h in range(HG):
                    dve.wait_ge(S("mix_hi_ready"), nth(l, DK, 4 + h + 1))
                    nc.vector.tensor_tensor(mix_lo[:, 4 + h, :], o_hg[:, h, :], mix_hi[:, 4 + h, :].bitcast(f32),
                                            ALU.subtract).then_inc(S("mix_ready"), 1)
                for j in range(0, DK, 2):
                    mix_low(l, S_OUT + j // 2)
                boundary(l, 1, g[:, G_NORM + 3 * DK:G_NORM + 4 * DK], g[:, G_NORM + 4 * DK:G_NORM + 5 * DK])

            dve.memset(ones[:, :], 1.0).then_inc(S("ones_ready"), 1)
            dve.memset(eps[:, :], EPS).then_inc(S("eps_ready"), 1)
            dve.wait_ge(S("gains_raw"), 32)
            dve.tensor_tensor(lmax[:, :], logit[:, 0, :], logit[:, 1, :], ALU.max).then_inc(S("lb_step"), 1)
            dve.wait_ge(S("lb_step"), 1)
            dve.tensor_tensor(e_logit[:, :, :], logit[:, :, :], lmax[:, :].unsqueeze(1).broadcast_to([P, L, HG]),
                              ALU.subtract).then_inc(S("lb_step"), 1)
            for k in range(DK):
                low_chunk(0, k, g_all[:, 0, k:k + 1])
            dve.wait_ge(S("lb_exp"), 1)
            dve.tensor_tensor(lsum[:, :], e_logit[:, 0, :], e_logit[:, 1, :], ALU.add).then_inc(S("lb_step"), 1)
            dve.wait_ge(S("lb_step"), 3)
            dve.reciprocal(lsum[:, :], lsum[:, :]).then_inc(S("lb_step"), 1)
            dve.wait_ge(S("lb_step"), 4)
            dve.tensor_tensor(e_logit[:, :, :], e_logit[:, :, :], lsum[:, :].unsqueeze(1).broadcast_to([P, L, HG]),
                              ALU.mult).then_inc(S("lb_step"), 1)
            dve.wait_ge(S("lb_step"), 5)
            dve.tensor_tensor(cum[:, :, :], e_logit[:, :, :], e_logit[:, 0, :].unsqueeze(1).broadcast_to([P, L, HG]),
                              ALU.add).then_inc(S("lb_step"), 1)
            dve.wait_ge(S("lb_step"), 6)
            dve.tensor_tensor(g_all[:, 1, G_LB:G_OML], cum[:, 1, :], e_logit[:, 0, :], ALU.subtract)
            dve.tensor_tensor(g_all[:, 0, G_LB:G_OML], e_logit[:, 0, :], e_logit[:, 0, :], ALU.subtract)\
                .then_inc(S("lb_step"), 1)
            dve.wait_ge(S("lb_step"), 7)
            dve.tensor_scalar(g_all[:, 0:L, G_OML:G_END], g_all[:, 0:L, G_LB:G_OML], -1.0, 1.0, ALU.mult, ALU.add)
            for n in (1, 5):
                cols = slice(G_NORM + n * DK, G_NORM + (n + 1) * DK)
                dve.tensor_scalar(g_all[:, 0:L, cols], g_all[:, 0:L, cols], 0.5, None, ALU.mult)
            dve.memset(g_all[:, L, 0:DK], 1.0).then_inc(S("lb_step"), 1)
            w_low(0, 0, 0, SLOT)
            dve.wait_ge(S("const_loaded"), 16 * 4)
            nc.vector.tensor_copy(mask[:, :, :], mask_raw[:, :, :]).then_inc(S("mask_ready"), 1)
            dve.wait_ge(S("mask_ready"), 1)
            with dve.Fori(0, L) as l:
                gate_up_phase(l, 0, GU_A)
                down_phase(l, 0, DOWN_A, SLOT)
                boundary(l, 0, g[:, G_NORM + DK:G_NORM + 2 * DK], g[:, G_NORM + 2 * DK:G_NORM + 3 * DK])
                mixer(l)
                gate_up_phase(l, 1, GU_B)
                down_phase(l, 1, DOWN_B, SLOT)
                boundary(l, 2, g[:, G_NORM + 5 * DK:G_NORM + 6 * DK], g_next)

        @block.gpsimd
        def _(pool):
            def norm_sum(before, k):
                pool.wait_ge(S("x_sq_ready"), before + (k + 1))
                if k == 1:
                    nc.gpsimd.tensor_tensor(x_acc[:, :], scr[:, 2, :], scr[:, 3, :], ALU.add)\
                        .then_inc(S("x_acc_ready"), 2)
                else:
                    pool.wait_ge(S("x_acc_ready"), before + k)
                    nc.gpsimd.tensor_tensor(x_acc[:, :], x_acc[:, :], scr[:, 2 + k % 6, :], ALU.add)\
                        .then_inc(S("x_acc_ready"), 1)

            def boundary(l, b):
                for k in range(6):
                    x_add(l, b, k)
                norm_sum(nth(l, 3 * DK, DK * (b + 1)), 1)
                x_add(l, b, 6)
                x_add(l, b, 7)
                for k in range(2, DK):
                    norm_sum(nth(l, 3 * DK, DK * (b + 1)), k)

            def x_add(l, b, k):
                pool.wait_ge(S("t_ready"), nth(l, 3 * DK, b * DK + k + 1))
                nc.gpsimd.tensor_tensor(x[:, k, :], x[:, k, :], scr[:, k % 2, :], ALU.add).then_inc(S("x_ready"), 1)

            def y_sum(l, b):
                base = b * DK
                pool.wait_ge(S("y_evac"), nth(l, 3 * DK, base + 4))
                nc.gpsimd.tensor_tensor(y_acc[:, :], scr[:, 0, :], scr[:, 1, :], ALU.add)\
                    .then_inc(S("y_acc_ready"), 2)
                with pool.Fori(1, DK // 2) as i:
                    for e in range(2):
                        pool.wait_ge(S("y_evac"), l * (3 * DK) + (i * 2 + (base + e + 3)))
                        pool.wait_ge(S("y_acc_ready"), l * (3 * DK) + (i * 2 + (base + e + 2)))
                        nc.gpsimd.tensor_tensor(y_acc[:, :], y_acc[:, :], scr[:, e, :], ALU.add)\
                            .then_inc(S("y_acc_ready"), 1)

            def gate_up_phase(l, f):
                with pool.Fori(0, HALF) as i:
                    for e in range(2):
                        t = l * (2 * FT) + (i * 2 + (f * FT + e))
                        pool.wait_ge(S("gu_evac"), t + 3)
                        pool.wait_ge(S("a_lo_ready"), t + 1)
                        pool.wait_ge(S("sg_ready"), t + 3)
                        nc.gpsimd.tensor_tensor(scr[:, 6 + e, :], scr[:, 4 + e, :], scr[:, 2 + e, :], ALU.mult)\
                            .then_inc(S("a_ready"), 1)

            def keys_up(l, v):
                half = LEVELS[v - 1]
                n_tot = v - 3
                pool.wait_ge(S("level_done"), nth(l, NLEV, v))
                if n_tot:
                    pool.wait_ge(S("hk_up"), nth(l, NLEV - 2, n_tot))
                    pool.wait_ge(S("tot_up"), nth(l, NLEV - 2, n_tot))
                if half < 64:
                    k = hk[:, :, :].rearrange("p h (n two s) -> p (h n) two s", two=2, s=half)[:, :, 0, :]
                    second = tot[half][:, :, :].rearrange("p h (n two) -> p (h n) two", two=2)[:, :, 1]
                    second = second.unsqueeze(2).broadcast_to([P, second.shape[1], half])
                else:
                    k = hk[:, :, 0:TP].rearrange("p h (n two s) -> p h n two s", two=2, s=half)[:, :, :, 0, :]
                    second = tot[half][:, :, 0:4].rearrange("p h (n two) -> p h n two", two=2)[:, :, :, 1]
                    second = second.unsqueeze(3).broadcast_to([P, HG, 2, half])
                nc.gpsimd.tensor_tensor(k, k, second, ALU.mult).then_inc(S("hk_up"), 1)

            def mixer(l):
                pool.wait_ge(S("rstd_ready"), nth(l, 3, 2))
                nc.gpsimd.tensor_tensor(scr[:, 0, :], cos[:, :], rstd[:, :], ALU.mult)
                nc.gpsimd.tensor_tensor(scr[:, 1, :], sin[:, :], rstd[:, :], ALU.mult).then_inc(S("cs_krr"), 1)
                pool.wait_ge(S("c_sq_ready"), nth(l, 5, 2))
                nc.gpsimd.tensor_tensor(c_acc[:, 0, :], c_sq[:, 0, :], c_sq[:, 1, :], ALU.add)\
                    .then_inc(S("c_acc_ready"), 2)
                pool.wait_ge(S("c_sq_ready"), nth(l, 5, 3))
                pool.wait_ge(S("c_acc_ready"), nth(l, 5, 2))
                nc.gpsimd.tensor_tensor(c_acc[:, 0, :], c_acc[:, 0, :], c_sq[:, 0, :], ALU.add)\
                    .then_inc(S("c_acc_ready"), 1)
                pool.wait_ge(S("c_sq_ready"), nth(l, 5, 5))
                nc.gpsimd.tensor_tensor(c_acc[:, 1, :], c_sq[:, 1, :], c_sq[:, 0, :], ALU.add)\
                    .then_inc(S("c_acc_ready"), 2)
                emptied(pool, l, ("m", M_KRS))
                nc.gpsimd.tensor_tensor(krr[:, :], kt1[:, :], kt2[:, :], ALU.add).then_inc(S("krr_ready"), 1)
                pool.wait_ge(S("cr_ready"), nth(l, 2, 1))
                nc.gpsimd.tensor_tensor(cos_r[:, :], cos[:, :], r_q[:, :], ALU.mult)
                nc.gpsimd.tensor_tensor(sin_r[:, :], sin[:, :], r_q[:, :], ALU.mult).then_inc(S("cs_q"), 1)
                for s in range(NG + 2):
                    if s - 2 in LAST_GROUP:
                        o_root(l, LAST_GROUP[s - 2])
                    v = s - FIRST_LEVEL_STEP
                    if 2 <= v < NLEV:
                        keys_up(l, v + 1)
                pool.wait_ge(S("hg_silu"), nth(l, 1, 1))
                for h in range(HG):
                    pool.wait_ge(S("o_t_ready"), nth(l, HG, h + 1))
                    nc.gpsimd.tensor_tensor(o_hg[:, h, :], o_hg[:, h, :], scr[:, 4 + h, :], ALU.mult)\
                        .then_inc(S("o_g_ready"), 1)

            def o_root(l, qt):
                nq = QT[qt][1]
                pool.wait_ge(S("o_var_ready"), nth(l, 3, qt + 1))
                nc.gpsimd.tensor_tensor(rn[0:nq, qt:qt + 1], sv[0:nq, qt:qt + 1], minus_half[0:nq, 0:1], ALU.pow)\
                    .then_inc(S("o_rn_ready"), 1)

            nc.gpsimd.memset(minus_half[:, :], -0.5)
            nc.gpsimd.memset(row_ind[:, 64:P], 0.0)
            nc.gpsimd.memset(row_ind[:, 0:64], 1.0)
            nc.gpsimd.memset(neg[:, :], -1e30).then_inc(S("ones_ready"), 1)
            for k in range(1, DK):
                norm_sum(0, k)
            pool.wait_ge(S("lb_step"), 8)
            with pool.Fori(0, L) as l:
                nc.gpsimd.tensor_copy(g[:, :], g_all[:, bass.ds(l, 1), :]).then_inc(S("gains_ready"), 1)
                gate_up_phase(l, 0)
                nc.gpsimd.tensor_copy(g_next[:, :], g_all[:, bass.ds(l + 1, 1), 0:DK]).then_inc(S("gains_ready"), 1)
                y_sum(l, 0)
                boundary(l, 0)
                mixer(l)
                y_sum(l, 1)
                boundary(l, 1)
                gate_up_phase(l, 1)
                y_sum(l, 2)
                boundary(l, 2)


def kernel(**inputs):
    import numpy as np
    import concourse.bacc as bacc
    from concourse.bass_utils import run_bass_kernel_spmd as run

    a = {n: np.asarray(v) for n, v in inputs.items()}

    def chunked(w, n):
        return w.reshape((L, n, P) + w.shape[2:]).swapaxes(1, 2)

    x = np.concatenate([a["x_prompt"][0], a["x_sample"][0]], axis=0)
    x_in = x.T.reshape(DK, P, T).transpose(1, 0, 2)
    per_layer = [a["norm_gains"].reshape(L, 6 * DK, P)] + [
        a[n].reshape(L, -1, P) for n in ("q_norm_gain", "kv_norm_gain", "mla_out_gain", "hg_norm_gain",
                                         "hg_lb_logits")]
    gains = np.concatenate(per_layer, axis=1).transpose(2, 0, 1)
    half = ROPE // 2
    inv = np.float32(10000.0) ** (-np.arange(half, dtype=np.float32) / np.float32(half))
    ang = (np.arange(T, dtype=np.float32)[:, None] * inv.astype(np.float32)).T
    cos_t = np.tile(np.cos(ang), (8, 1)).astype(np.float32)
    sin_t = np.tile(np.concatenate([-np.sin(ang), np.sin(ang)]), (4, 1)).astype(np.float32)
    mask = np.zeros((P, NLEV, 64), np.float32)
    q = np.arange(64)
    for v, hb in enumerate(LEVELS):
        t = 2 * q - hb if hb <= 0 else q // hb * 2 * hb + hb + q % hb
        key = np.arange(P)[:, None]
        mask[:, v, :] = key == t if hb <= 0 else key // hb == t // hb - 1

    def gate_up(w):
        return w.reshape(L, DK, P, 2, FT, P).transpose(0, 4, 2, 1, 3, 5).reshape(L, FT, P, SLOT)

    def down(w):
        return w.reshape(L, 2, HALF, P, DK, P).transpose(0, 4, 1, 3, 2, 5).reshape(L, 2 * DK, P, DOWN_W)

    def slots(w, rows, per_slot):
        n = w.shape[2] // (per_slot * P)
        w = w.reshape(L, rows, P, n, per_slot, P).transpose(0, 3, 2, 4, 1, 5).reshape(L, n, P, per_slot * rows * P)
        out = np.zeros((L, n, P, SLOT), w.dtype)
        out[..., :w.shape[3]] = w
        return out

    w_in = a["w_in"]
    c = CQ * P
    kr = w_in[:, :, c + CKV * P:c + CKV * P + ROPE]
    kr_swap = np.concatenate([kr[..., half:], kr[..., :half]], axis=-1)
    rest = w_in[:, :, c + CKV * P + ROPE:]
    n = HG * P
    hq, hf, rest = rest[..., :n], rest[..., n:2 * n], rest[..., 2 * n:]
    w_in = np.concatenate([w_in[:, :, :c + CKV * P]] + [kr] * 4 + [kr_swap] * 4 + [hf, hq, rest, rest[:, :, :P]],
                          axis=-1)
    s_in = slots(w_in, DK, 2)
    uq = a["w_uq"].reshape(L, CQ * P, H, QK)
    rope = uq[..., NOPE:]
    rope_swap = np.concatenate([rope[..., half:], rope[..., :half]], axis=-1)
    uq = np.concatenate([z.reshape(L, CQ * P, -1) for z in (uq[..., :NOPE], rope, rope_swap)], axis=-1)
    s_uq = slots(uq, CQ, 4)
    ukv = a["w_ukv"].reshape(L, CKV * P, H, NOPE + VD)
    s_kn = slots(ukv[..., :NOPE].reshape(L, CKV * P, H * NOPE), CKV, 4)
    v = ukv[..., NOPE:].reshape(L, 1, CKV, P, H * VD).transpose(0, 1, 3, 2, 4).reshape(L, 1, P, CKV * H * VD)
    s_v = np.zeros((L, 1, P, SLOT), v.dtype)
    s_v[..., :v.shape[3]] = v
    s_out = slots(a["w_out"], DK, 2)
    mix = np.concatenate([s_in[:, :6], s_uq, s_kn, s_v, s_in[:, 6:], s_out], axis=1)

    both = lambda x, y: np.stack([x, y], axis=1)
    given = {
        "x": x_in, "gains": gains, "cos": cos_t, "sin": sin_t, "ident": np.eye(P, dtype=np.float32), "mask": mask,
        "wgu": both(gate_up(a["ffa_w_gu"]), gate_up(a["ffb_w_gu"])).reshape(L * 2 * FT, P, SLOT),
        "wdn": both(down(a["ffa_w_down"]), down(a["ffb_w_down"])).reshape(L * 4 * DK, P, DOWN_W),
        "wmix": mix.reshape(L * MIX_SLOTS, P, SLOT),
        "latc": chunked(a["cache_mla_latent"][:, 0].swapaxes(1, 2), CKV),
        "krc": a["cache_mla_krope"][:, 0].swapaxes(1, 2),
        "s0": a["state_hgrn"][:, 0].transpose(0, 2, 1, 3),
    }
    nc = bacc.Bacc("TRN2", target_bir_lowering=False, num_devices=1)
    arrays, args = {}, []
    for name, arr in given.items():
        arr = np.ascontiguousarray(arr)
        arrays[f"in_{name}"] = arr
        args.append(nc.dram_tensor(f"in_{name}", arr.shape, mybir.dt.from_np(arr.dtype), kind="ExternalInput").ap())
    outs = {"x": (P, DK, T), "lat": (L, P, CKV, T), "kr": (L, ROPE, T), "st": (L, 2, P, HG, P)}
    for name, shape in outs.items():
        args.append(nc.dram_tensor(f"out_{name}", shape, mybir.dt.float32, kind="ExternalOutput").ap())
    trunk(nc, *args)
    r = run(nc, [arrays], core_ids=[0]).results[0]
    y = r["out_x"].transpose(2, 1, 0).reshape(T, D)
    lat = r["out_lat"].transpose(0, 3, 2, 1).reshape(L, T, CKV * P)
    kr = r["out_kr"].transpose(0, 2, 1)
    st = r["out_st"].transpose(0, 1, 3, 2, 4)
    return (y[None, :TP], y[None, TP:], lat[:, None, :TP], kr[:, None, :TP], st[:, 0][:, None],
            lat[:, None, TP:], kr[:, None, TP:], st[:, 1][:, None])
```

```python
import concourse.bass as bass
from concourse import mybir
from contextlib import ExitStack

P = 128
D = 1024
DK = D // P
TP, TS = 256, 64
T = TP + TS
PAST = 256
TB = 3
TOK = [0, 128, T - P]
TAKEN = [(0, P), (P, P), (2 * P, T - 2 * P)]
KEYS = T + PAST
L = 2
FF = 2816
FT = FF // P
HALF = FT // 2
H = 8
NOPE, ROPE, VD = 64, 32, 64
QK = NOPE + ROPE
SCALE = QK ** -0.5
HG = 4
EPS = 1e-6
CQ, CKV = 3, 2

GU_A, DOWN_A, MIX, GU_B, DOWN_B = 0, FT, FT + 2 * DK, 58, 58 + FT
SLOTS = 2 * (FT + 2 * DK) + 20
SLOT = 2048
DOWN_W = HALF * P
S_IN, S_UQ, S_KN, S_V, S_IN2, S_OUT = 0, 6, 8, 9, 10, 16
MIX_SLOTS = 20
MIX_WIDTH = [SLOT] * 6 + [1536] * 2 + [1024] * 2 + [SLOT] * 5 + [1024] + [SLOT] * 4
M_CQ, M_CKV, M_KR, M_KRS, M_HF, M_HQ, M_HI, M_HG, M_END = 0, 3, 5, 6, 7, 11, 15, 19, 23
M_FIRST = 12

G_NORM, G_Q, G_KV, G_MLA, G_HG, G_LB, G_OML, G_END = 0, 48, 51, 53, 57, 58, 62, 66

QT = [(0, 128, 0, 128), (128, 128, 0, 256), (256, 64, 256, 320)]
GROUPS = [(0, range(0, 4)), (0, range(4, 8))] + [(1, range(h, h + 2)) for h in range(0, H, 2)] \
    + [(2, range(h, h + 1)) for h in range(H)]
NG = len(GROUPS)
LAST_GROUP = {1: 0, 5: 1, 13: 2}
VBLK = [(0, 128), (128, 128), (256, 64), (320, 128), (448, 128)]
KBLK = {0: [(0, 0)], 1: [(0, 0), (1, 128)], 2: [(2, 0), (3, 64), (4, 192)]}

HBLK = [(0, 128), (128, 128), (256, 64)]
LEVELS = [0, -1, 1, 2, 4, 8, 16, 32, 64]
NLEV = len(LEVELS)
FIRST_LEVEL_STEP = 3

SUM_AT = 6
FIRST_CHUNKS = [(0, 0), (0, 1), (1, 0), (1, 1), (0, 2), (0, 3), (1, 2), (1, 3)] \
    + [(e, k) for e in range(2) for k in range(DK // 2, DK)]
OUT_BANK = [4, 5, 6, 7, 4, 5, 4, 5]
OUT_AFTER = {4: 0, 5: 1, 6: 4, 7: 5}


FREE_AT_START = ("split_done", "slot_used", "gu_evac", "sg_ready", "a_ready", "a_lo_ready", "y_evac", "y_acc_ready")


TILE_AT = {s: M_FIRST + n for n, s in enumerate([0, 1, 2, 3, 4, 5, 6, 7, 8, 10, 12])}
SPLIT_AT = {s: n for n, s in enumerate([0, 2, 4, 6, 8, 11])}
VT_AT = {8: 0, 9: 1, 10: 2}


def _jobs():
    jobs = []
    pre = [("m", m) for m in range(M_FIRST)] + [("uq", j) for j in range(8)] + [("kn", j) for j in range(8)] \
        + [("v", b) for b in range(5)]
    for n, job in enumerate(pre):
        act = job[0] == "v" or (job[0] == "kn" and job[1] % 2)
        jobs.append((job, n % 4, "act" if act else "dve"))
    steps = []
    for s in range(NG + 2):
        if s in TILE_AT:
            steps.append(("m", TILE_AT[s]))
        if s in VT_AT:
            steps.append(("vt", VT_AT[s]))
    for n, job in enumerate(steps):
        jobs.append((job, n % 2, "act" if job[0] == "vt" else "dve"))
    tail = [("kt", b) for b in range(3)] + [("st", b) for b in range(3)] + [("at", c) for c in range(4)] \
        + [("o", h) for h in range(HG)] + [("hn", 0)] + [("hs", h) for h in range(HG)]
    for n, job in enumerate(tail):
        jobs.append((job, n % 4, "act" if job[0] in ("kt", "hn") else "dve"))
    return jobs


JOBS = _jobs()
NJ = len(JOBS)
JOB = {job: q for q, (job, _, _) in enumerate(JOBS)}
BANK = {job: bank for job, bank, _ in JOBS}
N_EVAC = {e: sum(x == e for _, _, x in JOBS) for e in ("dve", "act")}


def _emptied(job):
    q = JOB[job]
    e = JOBS[q][2]
    return e, sum(x == e for _, _, x in JOBS[:q + 1])


FFN_SLOTS = SLOTS - MIX_SLOTS


def _ffn_slot(n):
    return n if n < MIX else n - MIX_SLOTS


def _last_job(s):
    if s < S_UQ:
        return "m", 2 * s + 1
    if s < S_IN2:
        return [("uq", 3), ("uq", 7), ("kn", 7), ("v", 4)][s - S_UQ]
    return "m", min(M_FIRST + 2 * (s - S_IN2) + 1, M_END - 1)


def _before(job):
    q = JOB[job]
    same = [j for j, b, _ in JOBS[:q] if b == BANK[job]]
    return same[-1] if same else None


def trunk(nc, x_in, gains_in, cos_in, sin_in, ident_in, mask_in, wgu_in, wdn_in, wmix_in, latc_in, krc_in, s0_in,
          x_out, lat_out, kr_out, st_out):
    f32, f32r, u8 = mybir.dt.float32, mybir.dt.float32r, mybir.dt.uint8
    ALU, ACT, AX = mybir.AluOpType, mybir.ActivationFunctionType, mybir.AxisListType
    nbytes = {f32: 4, f32r: 4, u8: 1}

    top = [(nc.sbuf_base + 31) // 32 * 32]
    start = {}

    def at(name, shape, dt, offset):
        n = nbytes[dt]
        for d in shape[1:]:
            n *= d
        start[name] = (offset, (n + 31) // 32 * 32)
        return nc.alloc_sbuf_tensor_at(name, shape, dt, offset=offset)

    def new(name, shape, dt=f32):
        t = at(name, shape, dt, top[0])
        top[0] += start[name][1]
        return t

    def over(first, *tensors):
        out = []
        for name, shape, dt in tensors:
            out.append(at(name, shape, dt, first))
            first += start[name][1]
        return out, first

    x = new("x", [P, DK, T])
    h_hi, h_lo = new("h_hi", [P, DK, T], f32r), new("h_lo", [P, DK, T], f32r)
    raw = [new(f"raw{i}", [P, SLOT]) for i in range(2)]
    w_hi = [new(f"w_hi{i}", [P, SLOT], f32r) for i in range(2)]
    w_lo = [new(f"w_lo{i}", [P, SLOT], f32r) for i in range(2)]
    cos, sin = new("cos", [P, T]), new("sin", [P, T])
    ident, ones = new("ident", [P, P]), new("ones", [P, P])
    mask = new("mask", [P, NLEV, 64], u8)
    row_ind, neg = new("row_ind", [1, P]), new("neg", [1, 64])
    row_ind_r, neg_r = new("row_ind_r", [1, P], f32r), new("neg_r", [1, 64], f32r)
    g_all, g = new("g_all", [P, L + 1, G_END]), new("g", [P, G_END])
    g_next = new("g_next", [P, DK])
    logit, e_logit = new("logit", [P, L, HG]), new("e_logit", [P, L, HG])
    lmax, lsum, cum = new("lmax", [P, HG]), new("lsum", [P, HG]), new("cum", [P, L, HG])
    y = new("y", [P, DK, T])
    scr = new("scr", [P, 8, T])
    rstd = new("rstd", [P, T])
    h_root, h_inv = new("h_root", [P, HG * TB]), new("h_inv", [P, HG * TB])
    root, inv_root, unread_root = new("root", [P, TB]), new("inv_root", [P, TB]), new("unread_root", [P, 4])
    y_acc, x_acc = new("y_acc", [P, T]), new("x_acc", [P, T])
    lat = new("lat", [P, CKV, KEYS])
    c_sq, c_acc = new("c_sq", [P, 2, T]), new("c_acc", [P, 2, T])
    krr = new("krr", [P, T])
    mx, nmx, rs, rinv = (new(n, [P, 3, H]) for n in ("mx", "nmx", "rs", "rinv"))
    ss, sv, rn = (new(n, [P, 3]) for n in ("ss", "sv", "rn"))
    minus_half, eps = new("minus_half", [P, 3]), new("eps", [P, 1])
    o_junk = new("o_junk", [P, H * VD])
    c_std = new("c_std", [P, 2, T])
    r_q, r_kv = new("r_q", [P, T]), new("r_kv", [P, T])
    shared = top[0]
    (a_hi, a_lo), _ = over(shared, ("a_hi", [P, FT, T], f32r), ("a_lo", [P, FT, T], f32r))
    (q_h, k_h, v_tok, hq, hk, f_gate), end = over(
        shared, ("q_h", [QK, H, T], f32), ("k_h", [QK, H, KEYS], f32), ("v_tok", [P, 5, H * VD], f32),
        ("hq", [P, HG, T], f32), ("hk", [P, HG, T], f32), ("f_gate", [P, HG, T], f32))
    tots, end = over(end, *[(f"tot{1 << i}", [P, HG, T >> i], f32) for i in range(1, 7)],
                     ("tot128", [P, HG, 2], f32))
    tot = {1: f_gate, **{1 << i: t for i, t in enumerate(tots, 1)}}
    cq_at = end
    (cq_hi, cq_lo), end = over(cq_at, ("cq_hi", [P, CQ, T], f32r), ("cq_lo", [P, CQ, T], f32r))
    (tri_p, tri_s, s0), _ = over(cq_at, ("tri_p", [P, 2 * HG, P], f32), ("tri_s", [64, HG, 64], f32),
                                 ("s0", [P, HG, P], f32))
    lat_at = end
    (lat_hi, lat_lo, cos_r, sin_r), end = over(lat_at, ("lat_hi", [P, CKV, KEYS], f32r),
                                               ("lat_lo", [P, CKV, KEYS], f32r),
                                               ("cos_r", [P, T], f32), ("sin_r", [P, T], f32))
    (pt, hv_tok), _ = over(lat_at, ("pt", [P, 2, 512], f32), ("hv_tok", [P, 3, HG * P], f32))
    assert end <= nc.sbuf_usable_end
    (hk_tok, s1, s2, s_smp, o_hg), _ = over(start["k_h"][0], ("hk_tok", [P, 3, HG * P], f32), ("s1", [P, HG, P], f32),
                                            ("s2", [P, HG, P], f32), ("s_smp", [P, HG, P], f32),
                                            ("o_hg", [P, HG, T], f32))
    (o_sq,), _ = over(start["q_h"][0], ("o_sq", [P, HG, T], f32))
    (c32, kt1, kt2), _ = over(start["y"][0], ("c32", [P, CQ + CKV, T], f32), ("kt1", [P, T], f32),
                              ("kt2", [P, T], f32))
    (mask_raw,), _ = over(start["y"][0], ("mask_raw", [P, NLEV, 64], f32))
    (o_att, prob), _ = over(start["y"][0], ("o_att", [P, 3, H * VD], f32), ("prob", [P, 2, 512], f32))
    mix_hi, mix_lo = h_hi, h_lo

    ctx = ExitStack()
    with ctx:
        bank = [ctx.enter_context(nc.psum_tensor(f"bank{i}", [P, 512], f32)) for i in range(8)]
        sem = {}

        def S(name):
            if name not in sem:
                sem[name] = ctx.enter_context(nc.semaphore(name))
            return sem[name]

        for name in ("x_half0 x_half1 logit_raw const_loaded raw_ready0 raw_ready1 hi_ready split_done slot_used gs_ready "
                     "gu_evac sg_ready a_ready a_hi_ready a_lo_ready out_done y_evac y_acc_ready y_sum_done "
                     "y_std_ready y_sq_last inv_ready bc_done t_ready x_ready h_hi_ready h_ready x_sq_ready x_acc_ready x_sum_done "
                     "x_std_ready rstd_ready ident_loaded gains_ready gains_raw lb_step ones_ready job_done job_evac_dve "
                     "job_evac_act h_inv_ready cs_krr krr_ready c_sq_ready c_acc_ready c_sum_done c_std_ready cr_ready "
                     "lat_ready cq_hi_ready cq_ready lat_hi_ready lat_lo_ready cs_q sig_ready "
                     "gate_ready q_rope_ready k_rope_ready score_done max_ready nmax_ready exp_ready ptr_done "
                     "pt_ready pv_done rinv_ready o_evac o_ss_ready o_var_ready o_rn_ready o_att_ready "
                     "tri_zero level_done level_evac hq_up hk_up tot_up hg_silu o_sq_ready "
                     "mix_hi_ready mix_ready latc_ready krc_ready s0_ready side_out "
                     "state_out y_out lb_exp eps_ready hi_half first_half mask_ready unread").split():
            S(name)
        block = ctx.enter_context(nc.Block())

        def nth(l, per_layer, n):
            return l * per_layer + n

        def wait_apart(eng, name, value):
            eng.wait_ge(S(name), value)
            eng.sem_inc(S("unread"), 1)

        def emptied(eng, l, job):
            e, n = _emptied(job)
            eng.wait_ge(S(f"job_evac_{e}"), nth(l, N_EVAC[e], n))

        def done(eng, l, job):
            eng.wait_ge(S("job_done"), nth(l, NJ, JOB[job] + 1))

        @block.sync
        def _(sp):
            sp.dma_start(g_all[:, 0:L, 0:G_LB], gains_in[:, :, 0:G_LB]).then_inc(S("gains_raw"), 16)
            sp.dma_start(logit[:, :, :], gains_in[:, :, G_LB:G_LB + HG]).then_inc(S("logit_raw"), 16)
            for name in FREE_AT_START:
                sp.sem_inc(S(name), 2)

            def load(l, n, par, dst, src):
                sp.wait_ge(S("split_done"), nth(l, SLOTS, n + 1))
                sp.dma_start(dst, src).then_inc(S(f"raw_ready{par}"), 16)

            def load_ffn(l, f, c0):
                with sp.Fori(0, FT // 2) as i:
                    for e in range(2):
                        load(l, i * 2 + (c0 + e), e, raw[e][:, :],
                             wgu_in[l * (2 * FT) + (i * 2 + (f * FT + e)), :, :])
                with sp.Fori(0, DK) as j:
                    for e in range(2):
                        load(l, j * 2 + (c0 + FT + e), e, raw[e][:, 0:DOWN_W],
                             wdn_in[l * (4 * DK) + (j * 2 + (f * 2 * DK + e)), :, :])

            with sp.Fori(0, L) as l:
                load_ffn(l, 0, GU_A)
                for s in range(MIX_SLOTS):
                    if s == 2:
                        sp.wait_ge(S("slot_used"), nth(l, FFN_SLOTS, MIX + 2))
                        for h in range(H):
                            sp.dma_start(k_h[NOPE:QK, h, T:KEYS], krc_in[l, :, :]).then_inc(S("krc_ready"), 16)
                        sp.dma_start(lat[:, :, T:KEYS], latc_in[l, :, :, :]).then_inc(S("latc_ready"), 16)
                    if s == S_IN2 + 1:
                        done(sp, l, ("uq", 7))
                        sp.dma_start(s0[:, :, :], s0_in[l, :, :, :]).then_inc(S("s0_ready"), 16)
                        sp.wait_ge(S("lat_ready"), nth(l, CKV, CKV))
                        sp.dma_start(lat_out[l, :, :, :], lat[:, :, 0:T]).then_inc(S("side_out"), 16)
                        sp.wait_ge(S("krr_ready"), nth(l, 1, 1))
                        sp.dma_start(kr_out[l, :, :], krr[0:ROPE, :]).then_inc(S("side_out"), 16)
                    if s == MIX_SLOTS - 1:
                        emptied(sp, l, ("st", 2))
                        sp.dma_start(st_out[l, 0, :, :, :], s2[:, :, :]).then_inc(S("state_out"), 16)
                        sp.dma_start(st_out[l, 1, :, :, :], s_smp[:, :, :]).then_inc(S("state_out"), 16)
                    w = MIX_WIDTH[s]
                    load(l, MIX + s, s % 2, raw[s % 2][:, 0:w], wmix_in[l * MIX_SLOTS + s, :, 0:w])
                load_ffn(l, 1, GU_B)
            for e in range(2):
                load(0, L * SLOTS + e, e, raw[e][:, 0:64], wgu_in[0, :, 0:64])
            for k in range(DK):
                sp.wait_ge(S("x_ready"), L * 3 * DK - DK + k + 1)
                sp.dma_start(x_out[:, k, :], x[:, k, :]).then_inc(S("y_out"), 16)
            sp.wait_ge(S("y_out"), 16 * DK)
            sp.wait_ge(S("side_out"), 32 * L)
            sp.wait_ge(S("state_out"), 32 * L)

        @block.tensor
        def _(pe):
            def split3(out, w, blk, m_w, rhs_hi, rhs_lo, first, last):
                hi, lo = w_hi[w][:, blk:blk + m_w], w_lo[w][:, blk:blk + m_w]
                nc.tensor.matmul(out, hi, rhs_hi, start=first, stop=False)
                nc.tensor.matmul(out, hi, rhs_lo, start=False, stop=False)
                return nc.tensor.matmul(out, lo, rhs_hi, start=False, stop=last)

            def pair(outs, w, blks, k, ready=None):
                if ready is not None:
                    pe.wait_ge(S("h_hi_ready"), ready)
                for part in (w_hi[w], w_lo[w]):
                    for out, blk in zip(outs, blks):
                        nc.tensor.matmul(out, part[:, blk:blk + P], h_hi[:, k, :], start=k == 0 and part is w_hi[w],
                                         stop=False)
                if ready is not None:
                    pe.wait_ge(S("h_ready"), ready)
                for out, blk in zip(outs, blks):
                    last = nc.tensor.matmul(out, w_hi[w][:, blk:blk + P], h_lo[:, k, :], start=False,
                                            stop=k == DK - 1)
                return last

            def slot(l, n):
                pe.wait_ge(S("split_done"), nth(l, SLOTS, n + 3))

            def gu_chunk(e, k, ready=None):
                return pair([bank[2 * e + i][:, 0:T] for i in range(2)], e, [(2 * k + i) * P for i in range(2)], k,
                            ready)

            def gu_tile(l, n, e, free):
                slot(l, n)
                pe.wait_ge(S("gu_evac"), free)
                for k in range(DK):
                    last = gu_chunk(e, k)
                last.then_inc(S("slot_used"), 1)

            def square_sums(out, squares):
                for i, t0 in enumerate(TOK):
                    last = nc.tensor.matmul(out[:, i:i + 1], squares[:, t0:t0 + P], ones[:, 0:1], start=True,
                                            stop=True)
                return last

            def keep_fast(n):
                for _ in range(n):
                    nc.tensor.matmul(bank[6][:, 0:P], ones[:, :], ident[:, :], start=True, stop=True)

            def x_sum(l, group):
                pe.wait_ge(S("x_acc_ready"), nth(l, 3 * DK, DK * (group + 1)))
                square_sums(bank[7], x_acc).then_inc(S("x_sum_done"), 1)

            def spread_factors(out, factors):
                for i, (t0, n) in enumerate(TAKEN):
                    last = nc.tensor.matmul(out[:, t0:t0 + n], factors[:, i:i + 1].broadcast_to([P, P]),
                                            ident[:, P - n:P], start=True, stop=True)
                return last

            def spread(l, n):
                pe.wait_ge(S("inv_ready"), nth(l, 6, n + 1))
                spread_factors(bank[7], inv_root).then_inc(S("bc_done"), 1)

            def gate_up_phase(l, f, c0):
                tb = f * FT
                group = 2 * f
                slot(l, c0)
                pe.wait_ge(S("gu_evac"), nth(l, 2 * FT, tb + 2))
                for e, k in FIRST_CHUNKS:
                    if (e, k) == (1, 0):
                        slot(l, c0 + 1)
                    last = gu_chunk(e, k, nth(l, 3 * DK, DK * group + k + 1) if e == 0 else None)
                    if k == DK - 1:
                        last.then_inc(S("slot_used"), 1)
                    if (e, k) == (0, SUM_AT):
                        x_sum(l, group)
                    if (e, k) == (0, DK - 1):
                        spread(l, 2 * group)
                with pe.Fori(1, FT // 2) as i:
                    for e in range(2):
                        gu_tile(l, i * 2 + (c0 + e), e, l * (2 * FT) + (i * 2 + (tb + e + 1)))

            def down_chunk(l, f, c, e, free, chunkwise):
                out = bank[4 + e][:, 0:T]
                for s in range(2):
                    slot(l, c + s)
                    if s == 0:
                        pe.wait_ge(S("y_evac"), free)
                    for kk in range(HALF):
                        k = s * HALF + kk
                        if chunkwise:
                            pe.wait_ge(S("a_lo_ready"), nth(l, 2 * FT, f * FT + k + 3))
                        last = split3(out, s, kk * P, P, a_hi[:, k, :], a_lo[:, k, :], k == 0, k == FT - 1)
                    last.then_inc(S("slot_used"), 1)

            def y_sum(l, b):
                keep_fast(5)
                pe.wait_ge(S("y_acc_ready"), nth(l, 3 * DK, DK * (b + 1) + 2))
                square_sums(bank[7], y_acc).then_inc(S("y_sum_done"), 1)
                keep_fast(3)
                spread(l, 2 * b + 1)
                keep_fast(8)

            def down_phase(l, f, c0):
                b = 2 * f
                down_chunk(l, f, c0, 0, nth(l, 3 * DK, b * DK + 1), True)
                with pe.Fori(0, 3) as i:
                    for e in range(2):
                        down_chunk(l, f, i * 4 + (c0 + 2 + 2 * e), 1 - e, l * (3 * DK) + (i * 2 + (b * DK + 2 + e)),
                                   False)
                down_chunk(l, f, c0 + 14, 1, nth(l, 3 * DK, b * DK + 8), False)
                y_sum(l, b)

            def begin(l, job):
                if _before(job) is not None:
                    emptied(pe, l, _before(job))
                return bank[BANK[job]]

            def m_tile(l, m, n, e):
                out = begin(l, ("m", m))[:, 0:T]
                if e == 0:
                    slot(l, MIX + n)
                for k in range(DK):
                    last = split3(out, n % 2, (e * DK + k) * P, P, h_hi[:, k, :], h_lo[:, k, :], k == 0, k == DK - 1)
                last.then_inc(S("job_done"), 1)

            def scores(l, n):
                qt, heads = GROUPS[n]
                q0, nq, k0, nk = QT[qt]
                if n >= 2:
                    pe.wait_ge(S("exp_ready"), nth(l, NG, n - 1))
                for i, h in enumerate(heads):
                    out = bank[2 + n % 2][0:nq, i * nk:(i + 1) * nk]
                    last = nc.tensor.matmul(out, q_h[:, h, q0:q0 + nq], k_h[:, h, k0:k0 + nk], start=True,
                                            stop=qt == 2)
                    if qt < 2:
                        last = nc.tensor.matmul(out[:, nk - 64:nk], row_ind_r[:, :], neg_r[:, :], start=False, stop=True)
                last.then_inc(S("score_done"), 1)

            def prob_transposes(l, n):
                qt, heads = GROUPS[n]
                q0, nq, k0, nk = QT[qt]
                if n >= 1:
                    pe.wait_ge(S("pt_ready"), nth(l, NG, n))
                wait_apart(pe, "exp_ready", nth(l, NG, n + 1))
                c = 0
                for i, h in enumerate(heads):
                    for b, off in KBLK[qt]:
                        kb = VBLK[b][1]
                        last = nc.tensor.transpose(bank[4][0:kb, c:c + nq],
                                                   prob[0:nq, n % 2, i * nk + off:i * nk + off + kb],
                                                   ident[0:nq, 0:nq])
                        c += nq
                last.then_inc(S("ptr_done"), 1)

            def values(l, n):
                qt, heads = GROUPS[n]
                q0, nq, k0, nk = QT[qt]
                if n in (2, 6):
                    pe.wait_ge(S("o_evac"), nth(l, 3, qt))
                wait_apart(pe, "pt_ready", nth(l, NG, n + 1))
                c = 0
                for h in heads:
                    for b, off in KBLK[qt]:
                        kb = VBLK[b][1]
                        last = nc.tensor.matmul(bank[5][0:nq, h * VD:(h + 1) * VD], pt[0:kb, n % 2, c:c + nq],
                                                v_tok[0:kb, b, h * VD:(h + 1) * VD], start=off == 0,
                                                stop=b == KBLK[qt][-1][0])
                        c += nq
                last.then_inc(S("pv_done"), 1)

            def level(l, v):
                half = LEVELS[v]
                if v == 0:
                    emptied(pe, l, ("m", M_HQ + 3))
                    pe.wait_ge(S("gate_ready"), nth(l, HG, HG))
                else:
                    pe.wait_ge(S("level_evac"), nth(l, NLEV, v))
                if v >= 2:
                    pe.wait_ge(S("hq_up"), nth(l, NLEV - 1, v - 1))
                if v >= 3:
                    pe.wait_ge(S("hk_up"), nth(l, NLEV - 2, v - 2))
                for b, (t0, nt) in enumerate(HBLK):
                    if half == 64 and b == 2:
                        continue
                    for h in range(HG):
                        q = hq[:, h, t0:t0 + nt]
                        if half <= 0:
                            q = q.rearrange("p (n two) -> p two n", two=2)[:, -half, :]
                        else:
                            q = q.rearrange("p (n two s) -> p two n s", two=2, s=half)[:, 1, :, :]
                        if b < 2:
                            out = bank[6][:, (b * HG + h) * 64:(b * HG + h + 1) * 64]
                        else:
                            out = bank[7][0:64, h * 32:(h + 1) * 32]
                        last = nc.tensor.matmul(out, hk[:, h, t0:t0 + nt], q, start=True, stop=True)
                last.then_inc(S("level_done"), 1)

            def head_transposes(l, job, src):
                t0, nt = HBLK[job[1]]
                e, n = _emptied(_before(job))
                wait_apart(pe, f"job_evac_{e}", nth(l, N_EVAC[e], n))
                out = bank[BANK[job]]
                for h in range(HG):
                    last = nc.tensor.transpose(out[0:nt, h * P:(h + 1) * P], src[:, h, t0:t0 + nt], ident[:, :])
                last.then_inc(S("job_done"), 1)

            def out_part(l, j, chunks):
                n = S_OUT + j // 2
                if j % 2 == 0 and chunks[0] == 0:
                    slot(l, MIX + n)
                for k in chunks:
                    if k < 4 and j == 0:
                        emptied(pe, l, ("at", k))
                    elif k >= 4 and j == 0:
                        pe.wait_ge(S("mix_ready"), nth(l, HG, k - 3))
                    last = split3(bank[OUT_BANK[j]][:, 0:T], n % 2, ((j % 2) * DK + k) * P, P, mix_hi[:, k, :],
                                  mix_lo[:, k, :], k == 0, k == DK - 1)
                if chunks[-1] == DK - 1:
                    last.then_inc(S("out_done"), 1)

            def mixer(l):
                slot(l, MIX)
                for n, k in FIRST_CHUNKS:
                    if (n, k) == (1, 0):
                        slot(l, MIX + 1)
                    last = pair([bank[BANK["m", 2 * n + e]][:, 0:T] for e in range(2)], n,
                                [(e * DK + k) * P for e in range(2)], k,
                                nth(l, 3 * DK, DK + k + 1) if n == 0 else None)
                    if k == DK - 1:
                        last.then_inc(S("job_done"), 2)
                    if (n, k) == (0, SUM_AT):
                        x_sum(l, 1)
                    if (n, k) == (0, DK - 1):
                        spread(l, 2)
                for n in range(2, S_UQ):
                    for e in range(2):
                        m = 2 * n + e
                        m_tile(l, m, n, e)
                        if m == M_KR:
                            pe.wait_ge(S("c_acc_ready"), nth(l, 5, 3))
                            nc.tensor.matmul(bank[6][:, 0:T], ones[:, :], c_acc[:, 0, :], start=True, stop=True)\
                                .then_inc(S("c_sum_done"), 1)
                        if m == M_HF:
                            pe.wait_ge(S("c_acc_ready"), nth(l, 5, 5))
                            nc.tensor.matmul(bank[5][:, 0:T], ones[:, :], c_acc[:, 1, :], start=True, stop=True)\
                                .then_inc(S("c_sum_done"), 1)
                for j in range(8):
                    out = begin(l, ("uq", j))[:, 0:T]
                    w = (S_UQ + j // 4) % 2
                    if j % 4 == 0:
                        slot(l, MIX + S_UQ + j // 4)
                    if j == 0:
                        pe.wait_ge(S("cq_ready"), nth(l, CQ, CQ))
                    for k in range(CQ):
                        last = split3(out, w, ((j % 4) * CQ + k) * P, P, cq_hi[:, k, :], cq_lo[:, k, :], k == 0,
                                      k == CQ - 1)
                    last.then_inc(S("job_done"), 1)
                slot(l, MIX + S_KN)
                pe.wait_ge(S("lat_lo_ready"), nth(l, 2, 2))
                for j in range(8):
                    out = begin(l, ("kn", j))[:, 0:KEYS // 2]
                    cols = slice((j % 2) * KEYS // 2, (j % 2 + 1) * KEYS // 2)
                    for k in range(CKV):
                        last = split3(out, S_KN % 2, ((j // 2) * CKV + k) * P, P, lat_hi[:, k, cols],
                                      lat_lo[:, k, cols], k == 0, k == CKV - 1)
                    last.then_inc(S("job_done"), 1)
                slot(l, MIX + S_V)
                for b, (k0, kb) in enumerate(VBLK):
                    out = begin(l, ("v", b))[0:kb, :]
                    for k in range(CKV):
                        hi, lo = (t[:, k, k0:k0 + kb] for t in (lat_hi, lat_lo))
                        w_h, w_l = (t[S_V % 2][:, k * 512:(k + 1) * 512] for t in (w_hi, w_lo))
                        nc.tensor.matmul(out, hi, w_h, start=k == 0, stop=False)
                        nc.tensor.matmul(out, hi, w_l, start=False, stop=False)
                        last = nc.tensor.matmul(out, lo, w_h, start=False, stop=k == CKV - 1)
                    last.then_inc(S("job_done"), 1)
                emptied(pe, l, ("v", 2))
                emptied(pe, l, ("v", 3))
                emptied(pe, l, ("kn", 6))
                pe.wait_ge(S("q_rope_ready"), nth(l, 1, 1))
                pe.wait_ge(S("k_rope_ready"), nth(l, 1, 1))
                pe.wait_ge(S("krc_ready"), nth(l, 16 * H, 16 * H))
                for s in range(NG + 2):
                    if s < NG:
                        scores(l, s)
                    if s in TILE_AT:
                        n = TILE_AT[s] - M_FIRST
                        m_tile(l, M_FIRST + n, S_IN2 + n // 2, n % 2)
                    if 1 <= s <= NG:
                        prob_transposes(l, s - 1)
                    if s >= 2:
                        values(l, s - 2)
                    if 0 <= s - FIRST_LEVEL_STEP < NLEV:
                        level(l, s - FIRST_LEVEL_STEP)
                    if s in VT_AT:
                        if VT_AT[s] == 0:
                            emptied(pe, l, ("m", M_HI + 3))
                        head_transposes(l, ("vt", VT_AT[s]), scr)
                pe.wait_ge(S("hk_up"), nth(l, NLEV - 2, NLEV - 2))
                for b in range(3):
                    head_transposes(l, ("kt", b), hk)
                for b, (t0, nt) in enumerate(HBLK):
                    out = begin(l, ("st", b))
                    emptied(pe, l, ("kt", b))
                    emptied(pe, l, ("vt", b))
                    for h in range(HG):
                        cols = slice(h * P, (h + 1) * P)
                        last = nc.tensor.matmul(out[:, cols], hk_tok[0:nt, b, cols], hv_tok[0:nt, b, cols],
                                                start=True, stop=True)
                    last.then_inc(S("job_done"), 1)
                pe.wait_ge(S("o_att_ready"), nth(l, 3, 3))
                for c in range(4):
                    out = begin(l, ("at", c))
                    for q0, nq, _, _ in QT:
                        qt = q0 // P
                        last = nc.tensor.transpose(out[:, q0:q0 + nq], o_att[0:nq, qt, c * P:(c + 1) * P],
                                                   ident[0:nq, 0:nq])
                    last.then_inc(S("job_done"), 1)
                pe.wait_ge(S("level_evac"), nth(l, NLEV, NLEV))
                pe.wait_ge(S("hq_up"), nth(l, NLEV - 1, NLEV - 1))
                pe.wait_ge(S("s0_ready"), nth(l, 16, 16))
                emptied(pe, l, ("st", 0))
                for h in range(HG):
                    out = begin(l, ("o", h))
                    cols = slice(h * P, (h + 1) * P)
                    nc.tensor.matmul(out[:, 0:128], hv_tok[:, 0, cols], tri_p[:, h, :], start=True, stop=True)
                    nc.tensor.matmul(out[:, 128:256], hv_tok[:, 1, cols], tri_p[:, HG + h, :], start=True, stop=False)
                    nc.tensor.matmul(out[:, 128:256], s1[:, h, :], hq[:, h, 128:256], start=False, stop=True)
                    nc.tensor.matmul(out[:, 256:320], hv_tok[0:64, 2, cols], tri_s[:, h, :], start=True, stop=False)
                    nc.tensor.matmul(out[:, 256:320], s0[:, h, :], hq[:, h, 256:320], start=False, stop=True)\
                        .then_inc(S("job_done"), 1)
                out_part(l, 0, range(4))
                out = begin(l, ("hn", 0))
                for h in range(HG):
                    out_part(l, 1, (h,))
                    pe.wait_ge(S("o_sq_ready"), nth(l, HG, h + 1))
                    last = square_sums(out[:, h * TB:(h + 1) * TB], o_sq[:, h, :])
                last.then_inc(S("job_done"), 1)
                out_part(l, 2, range(4))
                for h in range(HG):
                    out = begin(l, ("hs", h))
                    pe.wait_ge(S("h_inv_ready"), nth(l, 1, 1))
                    spread_factors(out, h_inv[:, h * TB:(h + 1) * TB]).then_inc(S("job_done"), 1)
                out_part(l, 3, range(4))
                for k in range(4, DK):
                    for j in range(2):
                        out_part(l, j, (k,))
                out_part(l, 2, range(4, DK))
                out_part(l, 3, range(4, DK))
                for j in range(4, DK):
                    pe.wait_ge(S("y_evac"), nth(l, 3 * DK, DK + OUT_AFTER[j] + 3))
                    out_part(l, j, range(DK))
                y_sum(l, 1)

            pe.wait_ge(S("ones_ready"), 3)
            pe.wait_ge(S("ident_loaded"), 16)
            with pe.Fori(0, L) as l:
                gate_up_phase(l, 0, GU_A)
                down_phase(l, 0, DOWN_A)
                mixer(l)
                gate_up_phase(l, 1, GU_B)
                down_phase(l, 1, DOWN_B)

        @block.scalar
        def _(act):
            act.dma_start(x[:, 0:4, :], x_in[:, 0:4, :]).then_inc(S("x_half0"), 16)
            act.dma_start(ident[:, :], ident_in).then_inc(S("ident_loaded"), 16)

            def slot_free(l, n, mixer_slot):
                if mixer_slot is None:
                    act.wait_ge(S("slot_used"), nth(l, FFN_SLOTS, n + 1))
                elif mixer_slot < S_OUT:
                    done(act, l, _last_job(mixer_slot))
                else:
                    act.wait_ge(S("out_done"), nth(l, DK, 2 * (mixer_slot - S_OUT) + 2))

            def w_high(l, n, par, w, mixer_slot=None, after_mixer=0):
                act.wait_ge(S(f"raw_ready{par}"), nth(l, 8 * SLOTS, (n - par) * 8 + 16))
                slot_free(l, n - after_mixer if mixer_slot is None else n, mixer_slot)
                nc.scalar.activation(w_hi[par][:, 0:w], raw[par][:, 0:w], ACT.Copy).then_inc(S("hi_ready"), 1)

            def high_half(l, b, half):
                n = (MIX, GU_B, SLOTS)[b] + 1
                cols = slice(half * SLOT // 2, (half + 1) * SLOT // 2)
                if half == 0:
                    act.wait_ge(S("raw_ready1"), nth(l, 8 * SLOTS, (n - 1) * 8 + 16))
                    if b == 1:
                        slot_free(l, n, MIX_SLOTS - 1)
                    else:
                        slot_free(l, _ffn_slot(n) if b == 2 else n, None)
                nc.scalar.activation(w_hi[1][:, cols], raw[1][:, cols], ACT.Copy)\
                    .then_inc(S("hi_ready" if half else "hi_half"), 1)

            def silu(t, e):
                act.wait_ge(S("gs_ready"), t + 1)
                act.wait_ge(S("a_ready"), t + 1)
                nc.scalar.activation(scr[:, 4 + e, :], scr[:, e, :], ACT.Silu).then_inc(S("sg_ready"), 1)

            def x_root(l, group):
                act.wait_ge(S("x_sum_done"), nth(l, 3, group + 1))
                nc.scalar.activation(root[:, :], bank[7][:, 0:TB], ACT.Sqrt, bias=eps[:, 0:1], scale=1.0 / D)\
                    .then_inc(S("x_std_ready"), 1)

            def norm_chunk(before, k, gain):
                nc.scalar.activation(h_hi[:, k, :], x[:, k, :], ACT.Copy, scale=gain).then_inc(S("h_hi_ready"), 1)
                if k >= 6:
                    act.wait_ge(S("x_acc_ready"), before + (k - 5))
                nc.scalar.activation(scr[:, 2 + k % 6, :], x[:, k, :], ACT.Square).then_inc(S("x_sq_ready"), 1)

            def evac_chunk(j, e, dst, gain, ended, count, last=False, bank_of=None):
                act.wait_ge(S("y_acc_ready"), j + 1)
                act.wait_ge(S(ended), count)
                src = bank[bank_of or 4 + e][:, 0:T]
                square = nc.scalar.activation(scr[:, e, :], src, ACT.Square)
                if last:
                    square.then_inc(S("y_sq_last"), 1)
                nc.scalar.activation(dst, src, ACT.Copy, scale=gain).then_inc(S("y_evac"), 1)

            def post_gain(b, j):
                c = G_NORM + (2 * b + 1) * DK
                return g[:, c + j:c + j + 1] if isinstance(j, int) else g[:, bass.ds(j + c, 1)]

            def boundary(l, b, gain):
                nc.scalar.activation(unread_root[:, b:b + 1], eps[:, 0:1], ACT.Sqrt)
                ended = ("out_done", nth(l, DK, DK)) if b == 1 else \
                    ("slot_used", nth(l, FFN_SLOTS, _ffn_slot((DOWN_A, None, DOWN_B)[b]) + 18))
                evac_chunk(nth(l, 3 * DK, b * DK + 7), 1, y[:, 7, :], post_gain(b, 7), *ended, last=True)
                high_half(l, b, 0)
                act.wait_ge(S("y_sum_done"), nth(l, 3, b + 1))
                nc.scalar.activation(root[:, :], bank[7][:, 0:TB], ACT.Sqrt, bias=eps[:, 0:1], scale=1.0 / D)\
                    .then_inc(S("y_std_ready"), 1)
                high_half(l, b, 1)
                for k in range(DK):
                    act.wait_ge(S("x_ready"), nth(l, 3 * DK, b * DK + k + 1))
                    norm_chunk(nth(l, 3 * DK, DK * (b + 1)), k, gain[:, k:k + 1])

            def gate_up_phase(l, f, c0):
                tb = f * FT
                am = MIX_SLOTS * f
                x_root(l, 2 * f)
                w_high(l, c0 + 2, 0, SLOT, None, am)
                silu(nth(l, 2 * FT, tb), 0)
                with act.Fori(1, HALF) as i:
                    for e in range(2):
                        w_high(l, i * 2 + (c0 + e + 1), 1 - e, SLOT, None, am)
                        silu(l * (2 * FT) + (i * 2 + (tb + e - 1)), 1 - e)

            def down_phase(l, f, c0, after):
                b, am = 2 * f, MIX_SLOTS * f
                w_high(l, c0 + 1, 1, DOWN_W, None, am)
                silu(nth(l, 2 * FT, f * FT + FT - 1), 1)
                w_high(l, c0 + 2, 0, DOWN_W, None, am)
                with act.Fori(0, 3) as i:
                    for e in range(2):
                        w_high(l, i * 4 + (c0 + 3 + 2 * e), 1, DOWN_W, None, am)
                        evac_chunk(l * (3 * DK) + (i * 2 + (b * DK + e)), e, y[:, bass.ds(i * 2 + e, 1), :],
                                   post_gain(b, i * 2 + e), "slot_used", l * FFN_SLOTS + (i * 4 + (_ffn_slot(c0) + 2 * e + 4)))
                        w_high(l, i * 4 + (c0 + 4 + 2 * e), 0, DOWN_W, None, am)
                w_high(l, c0 + 15, 1, DOWN_W, None, am)
                evac_chunk(nth(l, 3 * DK, b * DK + 6), 0, y[:, 6, :], post_gain(b, 6), "slot_used",
                           nth(l, FFN_SLOTS, _ffn_slot(c0) + 16))
                w_high(l, c0 + 16, 0, after, None, am)

            def mix_high(l, s):
                n = s + 1
                w_high(l, MIX + n, n % 2, MIX_WIDTH[n] if n < MIX_SLOTS else SLOT, n - 2 if n >= 2 else None)

            def c_square(l, j):
                act.wait_ge(S("job_evac_dve"), nth(l, N_EVAC["dve"], _emptied(("m", j))[1]))
                if j >= 2:
                    act.wait_ge(S("c_acc_ready"), nth(l, 5, j - 1))
                nc.scalar.activation(c_sq[:, j % 2, :], c32[:, j, :], ACT.Square).then_inc(S("c_sq_ready"), 1)

            def c_root(l, i):
                act.wait_ge(S("c_sum_done"), nth(l, 2, i + 1))
                nc.scalar.activation(c_std[:, i, :], bank[6 - i][:, 0:T], ACT.Sqrt, bias=eps[:, 0:1],
                                     scale=1.0 / (P * (CKV if i else CQ))).then_inc(S("c_std_ready"), 1)

            def sigmoids(l, j):
                act.wait_ge(S("job_evac_dve"), nth(l, N_EVAC["dve"], _emptied(("m", M_HF + j))[1]))
                if j >= 1:
                    act.wait_ge(S("gate_ready"), nth(l, HG, j))
                nc.scalar.activation(scr[:, 6, :], scr[:, 4 + j % 2, :], ACT.Sigmoid)
                nc.scalar.activation(scr[:, 7, :], scr[:, 4 + j % 2, :], ACT.Sigmoid, scale=-1.0)\
                    .then_inc(S("sig_ready"), 1)

            def exps(l, n):
                qt, heads = GROUPS[n]
                q0, nq, k0, nk = QT[qt]
                act.wait_ge(S("nmax_ready"), nth(l, NG, n + 1))
                if n >= 2:
                    act.wait_ge(S("ptr_done"), nth(l, NG, n - 1))
                for i, h in enumerate(heads):
                    last = nc.scalar.activation(prob[0:nq, n % 2, i * nk:(i + 1) * nk],
                                                bank[2 + n % 2][0:nq, i * nk:(i + 1) * nk], ACT.Exp,
                                                bias=nmx[0:nq, qt, h:h + 1], scale=SCALE,
                                                accum_out=rs[0:nq, qt, h:h + 1])
                last.then_inc(S("exp_ready"), 1)

            def att_square(l, qt):
                nq = QT[qt][1]
                act.wait_ge(S("o_evac"), nth(l, 3, qt + 1))
                nc.scalar.activation(o_junk[0:nq, :], o_att[0:nq, qt, :], ACT.Square, accum_out=ss[0:nq, qt:qt + 1])\
                    .then_inc(S("o_ss_ready"), 1)

            def evac(l, job, dst, src):
                done(act, l, job)
                nc.scalar.activation(dst, src, ACT.Copy).then_inc(S("job_evac_act"), 1)

            def mixer(l):
                for n in range(S_UQ):
                    if n == 0:
                        x_root(l, 1)
                    else:
                        mix_high(l, n)
                    if n in (1, 2):
                        c_square(l, 2 * n - 2)
                        c_square(l, 2 * n - 1)
                    if n == 3:
                        c_square(l, 4)
                        c_root(l, 0)
                        for k in range(CQ):
                            nc.scalar.activation(cq_hi[:, k, :], c32[:, k, :], ACT.Copy,
                                                 scale=g[:, G_Q + k:G_Q + k + 1]).then_inc(S("cq_hi_ready"), 1)
                    if n == 4:
                        c_root(l, 1)
                        sigmoids(l, 0)
                    if n == 5:
                        sigmoids(l, 1)
                        sigmoids(l, 2)
                act.wait_ge(S("latc_ready"), nth(l, 16, 16))
                nc.scalar.activation(lat_hi[:, :, T:KEYS], lat[:, :, T:KEYS], ACT.Copy).then_inc(S("lat_hi_ready"), 1)
                act.wait_ge(S("lat_ready"), nth(l, CKV, CKV))
                nc.scalar.activation(lat_hi[:, :, 0:T], lat[:, :, 0:T], ACT.Copy).then_inc(S("lat_hi_ready"), 1)
                sigmoids(l, 3)
                mix_high(l, S_UQ)
                act.wait_ge(S("krr_ready"), nth(l, 1, 1))
                nc.scalar.activation(k_h[NOPE:QK, :, 0:T], krr[NOPE:QK, :].unsqueeze(1).broadcast_to([ROPE, H, T]),
                                     ACT.Copy).then_inc(S("k_rope_ready"), 1)
                mix_high(l, S_UQ + 1)
                mix_high(l, S_KN)
                for j in range(1, 8, 2):
                    job = ("kn", j)
                    src = bank[BANK[job]]
                    cols = slice(KEYS // 2, KEYS)
                    done(act, l, job)
                    nc.scalar.activation(k_h[0:NOPE, j - 1, cols], src[0:NOPE, 0:KEYS // 2], ACT.Copy)
                    nc.scalar.activation(k_h[0:NOPE, j, cols], src[NOPE:P, 0:KEYS // 2], ACT.Copy)\
                        .then_inc(S("job_evac_act"), 1)
                mix_high(l, S_V)
                for b, (k0, kb) in enumerate(VBLK):
                    evac(l, ("v", b), v_tok[0:kb, b, :], bank[BANK["v", b]][0:kb, :])
                for s in range(NG + 2):
                    if s in SPLIT_AT and s < 11:
                        mix_high(l, S_IN2 + SPLIT_AT[s])
                    if s < NG:
                        exps(l, s)
                    if s == 11:
                        mix_high(l, S_IN2 + SPLIT_AT[s])
                    if s == NG:
                        act.wait_ge(S("job_evac_dve"), nth(l, N_EVAC["dve"], _emptied(("m", M_END - 1))[1]))
                        nc.scalar.activation(scr[:, 4:8, :], scr[:, 4:8, :], ACT.Silu).then_inc(S("hg_silu"), 1)
                    if s - 2 in LAST_GROUP:
                        att_square(l, LAST_GROUP[s - 2])
                    if s in VT_AT:
                        b = VT_AT[s]
                        nt = HBLK[b][1]
                        evac(l, ("vt", b), hv_tok[0:nt, b, :], bank[BANK["vt", b]][0:nt, :])
                for b, (t0, nt) in enumerate(HBLK):
                    evac(l, ("kt", b), hk_tok[0:nt, b, :], bank[BANK["kt", b]][0:nt, :])
                mix_high(l, S_OUT)
                for c in range(4):
                    done(act, l, ("at", c))
                    nc.scalar.activation(mix_hi[:, c, :], bank[BANK["at", c]][:, 0:T], ACT.Copy,
                                         scale=g[:, G_MLA + c:G_MLA + c + 1]).then_inc(S("mix_hi_ready"), 1)
                nc.scalar.activation(unread_root[:, 3:4], eps[:, 0:1], ACT.Sqrt)
                for h in range(HG):
                    job = ("o", h)
                    done(act, l, job)
                    nc.scalar.activation(o_sq[:, h, :], bank[BANK[job]][:, 0:T], ACT.Square)\
                        .then_inc(S("o_sq_ready"), 1)
                job = ("hn", 0)
                done(act, l, job)
                nc.scalar.activation(h_root[:, :], bank[BANK[job]][:, 0:HG * TB], ACT.Sqrt, bias=eps[:, 0:1],
                                     scale=1.0 / P).then_inc(S("job_evac_act"), 1)
                for h in range(HG):
                    emptied(act, l, ("hs", h))
                    nc.scalar.activation(mix_hi[:, 4 + h, :], o_hg[:, h, :], ACT.Copy).then_inc(S("mix_hi_ready"), 1)
                mix_high(l, S_OUT + 1)
                for j in range(DK - 1):
                    if j == 2:
                        mix_high(l, S_OUT + 2)
                    if j == 5:
                        mix_high(l, S_OUT + 3)
                    evac_chunk(nth(l, 3 * DK, DK + j), j % 2, y[:, j, :], post_gain(1, j), "out_done",
                               nth(l, DK, j + 1), bank_of=OUT_BANK[j])
                boundary(l, 1, g[:, G_NORM + 4 * DK:G_NORM + 5 * DK])

            act.wait_ge(S("gains_raw"), 16)
            act.wait_ge(S("eps_ready"), 1)
            act.wait_ge(S("x_half0"), 16)
            for k in range(DK):
                norm_chunk(0, k, g_all[:, 0, k:k + 1])
                if k == 0:
                    act.dma_start(x[:, 4:8, :], x_in[:, 4:8, :]).then_inc(S("x_half1"), 16)
                if k == 3:
                    act.wait_ge(S("raw_ready0"), 16)
                    for half in range(2):
                        cols = slice(half * SLOT // 2, (half + 1) * SLOT // 2)
                        nc.scalar.activation(w_hi[0][:, cols], raw[0][:, cols], ACT.Copy)\
                            .then_inc(S("hi_ready" if half else "first_half"), 1)
                    w_high(0, 1, 1, SLOT)
                    act.wait_ge(S("x_half1"), 16)
            act.wait_ge(S("lb_step"), 2)
            nc.scalar.activation(e_logit[:, :, :], e_logit[:, :, :], ACT.Exp).then_inc(S("lb_exp"), 1)
            nc.scalar.activation(unread_root[:, 3:4], eps[:, 0:1], ACT.Sqrt)
            act.dma_start(cos[:, :], cos_in).then_inc(S("const_loaded"), 16)
            act.dma_start(sin[:, :], sin_in).then_inc(S("const_loaded"), 16)
            act.dma_start(mask_raw[:, :, :], mask_in).then_inc(S("const_loaded"), 16)
            with act.Fori(0, L) as l:
                act.wait_ge(S("gains_ready"), nth(l, 2, 1))
                gate_up_phase(l, 0, GU_A)
                down_phase(l, 0, DOWN_A, SLOT)
                boundary(l, 0, g[:, G_NORM + 2 * DK:G_NORM + 3 * DK])
                mixer(l)
                gate_up_phase(l, 1, GU_B)
                down_phase(l, 1, DOWN_B, SLOT)
                boundary(l, 2, g_next)

        @block.vector
        def _(dve):
            def w_low(l, n, par, w):
                dve.wait_ge(S("hi_ready"), nth(l, SLOTS, n + 1))
                nc.vector.tensor_tensor(w_lo[par][:, 0:w], raw[par][:, 0:w], w_hi[par][:, 0:w].bitcast(f32),
                                        ALU.subtract).then_inc(S("split_done"), 1)

            def hidden_evac(t, e, used):
                dve.wait_ge(S("slot_used"), used)
                dve.wait_ge(S("sg_ready"), t + 1)
                nc.vector.tensor_tensor(scr[:, e, :], bank[2 * e][:, 0:T], rstd[:, :], ALU.mult)\
                    .then_inc(S("gs_ready"), 1)
                dve.wait_ge(S("a_ready"), t + 1)
                nc.vector.tensor_tensor(scr[:, 2 + e, :], bank[2 * e + 1][:, 0:T], rstd[:, :], ALU.mult)\
                    .then_inc(S("gu_evac"), 1)

            def hidden_split(t, e, dst_hi, dst_lo):
                dve.wait_ge(S("a_ready"), t + 3)
                nc.vector.tensor_scalar(dst_hi, scr[:, 6 + e, :], 1.0, None, ALU.mult).then_inc(S("a_hi_ready"), 1)
                dve.wait_ge(S("a_hi_ready"), t + 1)
                nc.vector.tensor_tensor(dst_lo, scr[:, 6 + e, :], dst_hi.bitcast(f32), ALU.subtract)\
                    .then_inc(S("a_lo_ready"), 1)

            def hg_low(l, h):
                dve.wait_ge(S("mix_hi_ready"), nth(l, DK, 4 + h + 1))
                nc.vector.tensor_tensor(mix_lo[:, 4 + h, :], o_hg[:, h, :], mix_hi[:, 4 + h, :].bitcast(f32),
                                        ALU.subtract).then_inc(S("mix_ready"), 1)

            def factors(l, n):
                nc.vector.reciprocal(inv_root[:, :], root[:, :]).then_inc(S("inv_ready"), 1)
                dve.wait_ge(S("bc_done"), nth(l, 6, n + 1))

            def add_last(acc, e, ready, count, squares, squared):
                dve.wait_ge(S(squares), squared)
                dve.wait_ge(S(ready), count - 1)
                nc.vector.tensor_tensor(acc[:, :], acc[:, :], scr[:, e, :], ALU.add).then_inc(S(ready), 1)

            def x_add_last(n0):
                add_last(x_acc, 2 + (DK - 1) % 6, "x_acc_ready", n0 + DK, "x_sq_ready", n0 + DK)

            def x_factor(l, group):
                dve.wait_ge(S("x_std_ready"), nth(l, 3, group + 1))
                factors(l, 2 * group)
                nc.vector.tensor_copy(rstd[:, :], bank[7][:, 0:T]).then_inc(S("rstd_ready"), 1)
                dve.wait_ge(S("rstd_ready"), nth(l, 3, group + 1))

            def low_chunk(before, k, gain):
                dve.wait_ge(S("h_hi_ready"), before + (k + 1))
                nc.vector.scalar_tensor_tensor(h_lo[:, k, :], x[:, k, :], gain, h_hi[:, k, :].bitcast(f32), ALU.mult,
                                               ALU.subtract).then_inc(S("h_ready"), 1)

            def boundary(l, b, pre):
                add_last(y_acc, 1, "y_acc_ready", nth(l, 3 * DK, DK * (b + 1) + 2), "y_sq_last", nth(l, 3, b + 1))
                dve.wait_ge(S("y_std_ready"), nth(l, 3, b + 1))
                factors(l, 2 * b + 1)
                t0, n0 = nth(l, 3 * DK, b * DK), nth(l, 3 * DK, DK * (b + 1))

                def t(k):
                    if k >= 2:
                        dve.wait_ge(S("x_ready"), t0 + (k - 1))
                    nc.vector.tensor_tensor(scr[:, k % 2, :], y[:, k, :], bank[7][:, 0:T], ALU.mult)\
                        .then_inc(S("t_ready"), 1)

                def add(k):
                    dve.wait_ge(S("t_ready"), t0 + (k + 1))
                    nc.vector.tensor_tensor(x[:, k, :], x[:, k, :], scr[:, k % 2, :], ALU.add)\
                        .then_inc(S("x_ready"), 1)

                t(0)
                add(0)
                t(1)
                add(1)
                low_chunk(n0, 0, pre[:, 0:1])
                for k in range(2, DK):
                    t(k)
                    if k % 2 == 0:
                        low_chunk(n0, k - 1, pre[:, k - 1:k])
                        add(k)
                    else:
                        add(k)
                        low_chunk(n0, k - 1, pre[:, k - 1:k])
                low_chunk(n0, DK - 1, pre[:, DK - 1:DK])
                x_add_last(n0)

            def gate_up_phase(l, f, c0):
                tb = f * FT
                x_factor(l, 2 * f)
                hidden_evac(nth(l, 2 * FT, tb), 0, nth(l, FFN_SLOTS, _ffn_slot(c0) + 3))
                dve.wait_ge(S("split_done"), nth(l, SLOTS, c0 + 4))
                w_low(l, c0 + 2, 0, SLOT)
                if f == 1:
                    dve.wait_ge(S("state_out"), nth(l, 32, 32))
                hidden_split(nth(l, 2 * FT, tb), 0, a_hi[:, 0, :], a_lo[:, 0, :])
                with dve.Fori(1, HALF) as i:
                    for e in range(2):
                        t = l * (2 * FT) + (i * 2 + (tb + e - 1))
                        hidden_evac(t, 1 - e, l * FFN_SLOTS + (i * 2 + (_ffn_slot(c0) + e + 2)))
                        w_low(l, i * 2 + (c0 + e + 1), 1 - e, SLOT)
                        at = bass.ds(i * 2 + (e - 1), 1)
                        hidden_split(t, 1 - e, a_hi[:, at, :], a_lo[:, at, :])

            def down_phase(l, f, c0, after):
                t = nth(l, 2 * FT, f * FT + FT - 1)
                hidden_evac(t, 1, nth(l, FFN_SLOTS, _ffn_slot(c0) + 2))
                w_low(l, c0 + 1, 1, DOWN_W)
                hidden_split(t, 1, a_hi[:, FT - 1, :], a_lo[:, FT - 1, :])
                w_low(l, c0 + 2, 0, DOWN_W)
                with dve.Fori(0, 6) as i:
                    w_low(l, i * 2 + (c0 + 3), 1, DOWN_W)
                    w_low(l, i * 2 + (c0 + 4), 0, DOWN_W)
                w_low(l, c0 + 15, 1, DOWN_W)
                w_low(l, c0 + 16, 0, after)

            def mix_low(l, s):
                n = s + 1
                w_low(l, MIX + n, n % 2, MIX_WIDTH[n] if n < MIX_SLOTS else SLOT)

            def m_evac(l, m):
                job = ("m", m)
                src = bank[BANK[job]][:, 0:T]
                if m in (M_KR, M_KRS):
                    dve.wait_ge(S("cs_krr"), nth(l, 1, 1))
                    dst, factor = (kt1, scr[:, 0, :]) if m == M_KR else (kt2, scr[:, 1, :])
                    dst = dst[:, :]
                else:
                    factor = rstd[:, :]
                    j = m - M_HF
                    if m < M_KR:
                        dst = c32[:, m, :]
                    elif m < M_HQ:
                        dst = scr[:, 4 + j % 2, :]
                        if j >= 2:
                            dve.wait_ge(S("sig_ready"), nth(l, HG, j - 1))
                    elif m < M_HI:
                        dst = hq[:, m - M_HQ, :]
                    else:
                        dst = scr[:, m - M_HI, :]
                done(dve, l, job)
                nc.vector.tensor_tensor(dst, src, factor, ALU.mult).then_inc(S("job_evac_dve"), 1)

            def gates(l, j):
                dve.wait_ge(S("sig_ready"), nth(l, HG, j + 1))
                nc.vector.tensor_scalar(f_gate[:, j, :], scr[:, 6, :], g[:, G_OML + j:G_OML + j + 1],
                                        g[:, G_LB + j:G_LB + j + 1], ALU.mult, ALU.add)
                nc.vector.tensor_scalar(hk[:, j, :], scr[:, 7, :], g[:, G_OML + j:G_OML + j + 1], None, ALU.mult)\
                    .then_inc(S("gate_ready"), 1)

            def group_max(l, n):
                qt, heads = GROUPS[n]
                q0, nq, k0, nk = QT[qt]
                hs = slice(heads[0], heads[-1] + 1)
                dve.wait_ge(S("score_done"), nth(l, NG, n + 1))
                nc.vector.tensor_reduce(mx[0:nq, qt, hs],
                                        bank[2 + n % 2][0:nq, 0:len(heads) * nk].rearrange("p (h k) -> p h k", k=nk),
                                        AX.X, ALU.max).then_inc(S("max_ready"), 1)
                dve.wait_ge(S("max_ready"), nth(l, NG, n + 1))
                nc.vector.tensor_scalar(nmx[0:nq, qt, hs], mx[0:nq, qt, hs], -SCALE, None, ALU.mult)\
                    .then_inc(S("nmax_ready"), 1)

            def pt_evac(l, n):
                qt, heads = GROUPS[n]
                dve.wait_ge(S("ptr_done"), nth(l, NG, n + 1))
                if n >= 2:
                    dve.wait_ge(S("pv_done"), nth(l, NG, n - 1))
                if qt < 2:
                    nc.vector.tensor_copy(pt[:, n % 2, :], bank[4][:, :]).then_inc(S("pt_ready"), 1)
                else:
                    nc.vector.tensor_copy(pt[0:64, n % 2, 0:64], bank[4][0:64, 0:64])
                    nc.vector.tensor_copy(pt[:, n % 2, 64:192], bank[4][:, 64:192]).then_inc(S("pt_ready"), 1)

            def o_evac(l, n):
                qt = LAST_GROUP[n]
                nq = QT[qt][1]
                dve.wait_ge(S("exp_ready"), nth(l, NG, n + 1))
                nc.vector.reciprocal(rinv[0:nq, qt, :], rs[0:nq, qt, :]).then_inc(S("rinv_ready"), 1)
                dve.wait_ge(S("rinv_ready"), nth(l, 3, qt + 1))
                dve.wait_ge(S("pv_done"), nth(l, NG, n + 1))
                nc.vector.tensor_tensor(o_att[0:nq, qt, :].rearrange("p (h d) -> p h d", d=VD),
                                        bank[5][0:nq, :].rearrange("p (h d) -> p h d", d=VD),
                                        rinv[0:nq, qt, :].unsqueeze(2).broadcast_to([nq, H, VD]), ALU.mult)\
                    .then_inc(S("o_evac"), 1)

            def o_var(l, qt):
                nq = QT[qt][1]
                dve.wait_ge(S("o_ss_ready"), nth(l, 3, qt + 1))
                nc.vector.tensor_scalar(sv[0:nq, qt:qt + 1], ss[0:nq, qt:qt + 1], 1.0 / (H * VD), EPS, ALU.mult,
                                        ALU.add).then_inc(S("o_var_ready"), 1)

            def o_scale(l, qt):
                nq = QT[qt][1]
                dve.wait_ge(S("o_rn_ready"), nth(l, 3, qt + 1))
                nc.vector.tensor_scalar(o_att[0:nq, qt, :], o_att[0:nq, qt, :], rn[0:nq, qt:qt + 1], None, ALU.mult)\
                    .then_inc(S("o_att_ready"), 1)

            def tri_view(t, half):
                if half <= 0:
                    return t.rearrange("p u (n two) -> p two u n", two=2)[:, -half, :, :]
                return t.rearrange("p u (n two s) -> p two u n s", two=2, s=half)[:, 1, :, :, :]

            def level_evac(l, v):
                half = LEVELS[v]
                wait_apart(dve, "level_done", nth(l, NLEV, v + 1))
                for t, src, nk, units, nq in ((tri_p[:, :, :], bank[6], P, 2 * HG, 64), (tri_s[:, :, :], bank[7], 64, HG, 32)):
                    if half == 64 and nq == 32:
                        continue
                    m = mask[0:nk, v, 0:nq]
                    d = src[0:nk, 0:units * nq]
                    if half <= 0:
                        m = m.unsqueeze(1).broadcast_to([nk, units, nq])
                        d = d.rearrange("p (u n) -> p u n", n=nq)
                    else:
                        m = m.rearrange("p (n s) -> p n s", s=half).unsqueeze(1)\
                            .broadcast_to([nk, units, nq // half, half])
                        d = d.rearrange("p (u n s) -> p u n s", n=nq // half, s=half)
                    last = nc.vector.copy_predicated(tri_view(t, half), m, d)
                last.then_inc(S("level_evac"), 1)

            def pairs(t, half):
                return t[:, :, :].rearrange("p h (n two s) -> p (h n) two s", two=2, s=half)

            def queries_up(l, v):
                dve.wait_ge(S("level_done"), nth(l, NLEV, v))
                if v == 2:
                    nc.vector.tensor_tensor(hq[:, :, :], hq[:, :, :], f_gate[:, :, :], ALU.mult)\
                        .then_inc(S("hq_up"), 1)
                    dve.wait_ge(S("hq_up"), nth(l, NLEV - 1, 1))
                    return
                half = LEVELS[v - 1]
                n_tot = v - 3
                dve.wait_ge(S("hq_up"), nth(l, NLEV - 1, v - 2))
                if n_tot:
                    dve.wait_ge(S("tot_up"), nth(l, NLEV - 2, n_tot))
                if half < 64:
                    q = pairs(hq, half)[:, :, 1, :]
                    two = tot[half][:, :, :].rearrange("p h (n two) -> p (h n) two", two=2)
                    first, second = two[:, :, 0], two[:, :, 1]
                    n = first.shape[1]
                    nc.vector.tensor_tensor(q, q, first.unsqueeze(2).broadcast_to([P, n, half]), ALU.mult)\
                        .then_inc(S("hq_up"), 1)
                    up = tot[2 * half][:, :, :].rearrange("p h n -> p (h n)")
                else:
                    q = hq[:, :, 0:TP].rearrange("p h (n two s) -> p h n two s", two=2, s=half)[:, :, :, 1, :]
                    two = tot[half][:, :, 0:4].rearrange("p h (n two) -> p h n two", two=2)
                    first, second = two[:, :, :, 0], two[:, :, :, 1]
                    nc.vector.tensor_tensor(q, q, first.unsqueeze(3).broadcast_to([P, HG, 2, half]), ALU.mult)\
                        .then_inc(S("hq_up"), 1)
                    up = tot[128][:, :, :]
                nc.vector.tensor_tensor(up, first, second, ALU.mult).then_inc(S("tot_up"), 1)

            def mixer(l):
                x_factor(l, 1)
                m_evac(l, 0)
                m_evac(l, 1)
                dve.wait_ge(S("split_done"), nth(l, SLOTS, MIX + 4))
                mix_low(l, 1)
                m_evac(l, 2)
                m_evac(l, 3)
                mix_low(l, 2)
                m_evac(l, 4)
                m_evac(l, M_KR)
                mix_low(l, 3)
                m_evac(l, M_KRS)
                dve.wait_ge(S("c_std_ready"), nth(l, 2, 1))
                nc.vector.reciprocal(r_q[:, :], c_std[:, 0, :]).then_inc(S("cr_ready"), 1)
                for k in range(CQ):
                    dve.wait_ge(S("cq_hi_ready"), nth(l, CQ, k + 1))
                    nc.vector.scalar_tensor_tensor(cq_lo[:, k, :], c32[:, k, :], g[:, G_Q + k:G_Q + k + 1],
                                                   cq_hi[:, k, :].bitcast(f32), ALU.mult, ALU.subtract)\
                        .then_inc(S("cq_ready"), 1)
                m_evac(l, M_HF)
                mix_low(l, 4)
                m_evac(l, M_HF + 1)
                dve.wait_ge(S("c_std_ready"), nth(l, 2, 2))
                nc.vector.reciprocal(r_kv[:, :], c_std[:, 1, :]).then_inc(S("cr_ready"), 1)
                dve.wait_ge(S("cr_ready"), nth(l, 2, 2))
                for k in range(CKV):
                    nc.vector.scalar_tensor_tensor(lat[:, k, 0:T], c32[:, CQ + k, :], g[:, G_KV + k:G_KV + k + 1],
                                                   r_kv[:, :], ALU.mult, ALU.mult).then_inc(S("lat_ready"), 1)
                gates(l, 0)
                m_evac(l, M_HF + 2)
                mix_low(l, 5)
                gates(l, 1)
                m_evac(l, M_HF + 3)
                gates(l, 2)
                m_evac(l, M_HQ)
                for i, cols in enumerate((slice(T, KEYS), slice(0, T))):
                    dve.wait_ge(S("lat_hi_ready"), nth(l, 2, i + 1))
                    nc.vector.tensor_tensor(lat_lo[:, :, cols], lat[:, :, cols], lat_hi[:, :, cols].bitcast(f32),
                                            ALU.subtract).then_inc(S("lat_lo_ready"), 1)
                gates(l, 3)
                mix_low(l, S_UQ)
                dve.wait_ge(S("cs_q"), nth(l, 1, 1))
                for j in range(8):
                    if j == 4:
                        mix_low(l, S_UQ + 1)
                    job = ("uq", j)
                    src = bank[BANK[job]]
                    done(dve, l, job)
                    if j < 4:
                        nc.vector.tensor_tensor(q_h[0:NOPE, 2 * j, :], src[0:NOPE, 0:T], r_q[0:NOPE, :], ALU.mult)
                        ins = nc.vector.tensor_tensor(q_h[0:NOPE, 2 * j + 1, :], src[NOPE:P, 0:T], r_q[NOPE:P, :],
                                                      ALU.mult)
                    else:
                        ins = nc.vector.tensor_tensor(scr[:, j - 4, :], src[:, 0:T],
                                                      (cos_r if j < 6 else sin_r)[:, :], ALU.mult)
                    ins.then_inc(S("job_evac_dve"), 1)
                for j in range(0, 8, 2):
                    if j == 4:
                        mix_low(l, S_KN)
                    job = ("kn", j)
                    src = bank[BANK[job]]
                    done(dve, l, job)
                    nc.vector.tensor_copy(k_h[0:NOPE, j, 0:KEYS // 2], src[0:NOPE, 0:KEYS // 2])
                    nc.vector.tensor_copy(k_h[0:NOPE, j + 1, 0:KEYS // 2], src[NOPE:P, 0:KEYS // 2])\
                        .then_inc(S("job_evac_dve"), 1)
                for h in range(H):
                    rows = slice(h % 4 * ROPE, (h % 4 + 1) * ROPE)
                    ins = nc.vector.tensor_tensor(q_h[NOPE:QK, h, :], scr[rows, h // 4, :], scr[rows, 2 + h // 4, :],
                                                  ALU.add)
                ins.then_inc(S("q_rope_ready"), 1)
                mix_low(l, S_V)
                dve.wait_ge(S("tri_zero"), nth(l, 1, 1))
                for s in range(NG + 2):
                    if s < NG:
                        group_max(l, s)
                    if s in SPLIT_AT and s < 11:
                        mix_low(l, S_IN2 + SPLIT_AT[s])
                    if s in TILE_AT:
                        m_evac(l, TILE_AT[s])
                    if 1 <= s <= NG:
                        pt_evac(l, s - 1)
                    if s == 11:
                        mix_low(l, S_IN2 + SPLIT_AT[s])
                    if s - 2 in LAST_GROUP:
                        o_evac(l, s - 2)
                        o_var(l, LAST_GROUP[s - 2])
                    if s - 3 in LAST_GROUP:
                        o_scale(l, LAST_GROUP[s - 3])
                    v = s - FIRST_LEVEL_STEP
                    if 0 <= v < NLEV:
                        level_evac(l, v)
                        if v >= 1:
                            queries_up(l, v + 1)
                o_scale(l, 2)
                for b in range(3):
                    job = ("st", b)
                    src = bank[BANK[job]]
                    done(dve, l, job)
                    if b == 0:
                        ins = nc.vector.tensor_copy(s1[:, :, :], src[:, :].rearrange("p (h d) -> p h d", h=HG))
                    else:
                        dve.wait_ge(S("tot_up"), nth(l, NLEV - 2, NLEV - 2))
                        if b == 1:
                            emptied(dve, l, ("st", 0))
                        else:
                            dve.wait_ge(S("s0_ready"), nth(l, 16, 16))
                        for h in range(HG):
                            before, after = (s1, s2) if b == 1 else (s0, s_smp)
                            decay = tot[128][:, h, 1:2] if b == 1 else tot[64][:, h, 4:5]
                            ins = nc.vector.scalar_tensor_tensor(after[:, h, :], before[:, h, :], decay,
                                                                 src[:, h * P:(h + 1) * P], ALU.mult, ALU.add)
                    ins.then_inc(S("job_evac_dve"), 1)
                for c in range(4):
                    dve.wait_ge(S("mix_hi_ready"), nth(l, DK, c + 1))
                    nc.vector.scalar_tensor_tensor(mix_lo[:, c, :], bank[BANK["at", c]][:, 0:T],
                                                   g[:, G_MLA + c:G_MLA + c + 1], mix_hi[:, c, :].bitcast(f32),
                                                   ALU.mult, ALU.subtract).then_inc(S("job_evac_dve"), 1)
                mix_low(l, S_OUT)
                dve.wait_ge(S("hg_silu"), nth(l, 1, 1))
                for h in range(HG):
                    dve.wait_ge(S("o_sq_ready"), nth(l, HG, h + 1))
                    nc.vector.scalar_tensor_tensor(o_hg[:, h, :], bank[BANK["o", h]][:, 0:T], g[:, G_HG:G_HG + 1],
                                                   scr[:, 4 + h, :], ALU.mult, ALU.mult)\
                        .then_inc(S("job_evac_dve"), 1)
                emptied(dve, l, ("hn", 0))
                nc.vector.reciprocal(h_inv[:, :], h_root[:, :]).then_inc(S("h_inv_ready"), 1)
                for h in range(HG):
                    job = ("hs", h)
                    done(dve, l, job)
                    nc.vector.tensor_tensor(o_hg[:, h, :], o_hg[:, h, :], bank[BANK[job]][:, 0:T], ALU.mult)\
                        .then_inc(S("job_evac_dve"), 1)
                    if h >= 1:
                        hg_low(l, h - 1)
                hg_low(l, HG - 1)
                for n in range(1, 4):
                    mix_low(l, S_OUT + n)
                boundary(l, 1, g[:, G_NORM + 4 * DK:G_NORM + 5 * DK])

            dve.memset(ones[:, :], 1.0).then_inc(S("ones_ready"), 1)
            dve.memset(eps[:, :], EPS).then_inc(S("eps_ready"), 1)
            dve.wait_ge(S("ones_ready"), 2)
            nc.vector.tensor_copy(row_ind_r[:, :], row_ind[:, :])
            nc.vector.tensor_copy(neg_r[:, :], neg[:, :]).then_inc(S("ones_ready"), 1)
            dve.wait_ge(S("gains_raw"), 16)
            dve.wait_ge(S("logit_raw"), 16)
            dve.tensor_tensor(lmax[:, :], logit[:, 0, :], logit[:, 1, :], ALU.max).then_inc(S("lb_step"), 1)
            dve.wait_ge(S("lb_step"), 1)
            dve.tensor_tensor(e_logit[:, :, :], logit[:, :, :], lmax[:, :].unsqueeze(1).broadcast_to([P, L, HG]),
                              ALU.subtract).then_inc(S("lb_step"), 1)
            for k in range(DK):
                if k == 4:
                    for half in range(2):
                        cols = slice(half * SLOT // 2, (half + 1) * SLOT // 2)
                        dve.wait_ge(S("hi_ready" if half else "first_half"), 1)
                        low = nc.vector.tensor_tensor(w_lo[0][:, cols], raw[0][:, cols],
                                                      w_hi[0][:, cols].bitcast(f32), ALU.subtract)
                    low.then_inc(S("split_done"), 1)
                    w_low(0, 1, 1, SLOT)
                low_chunk(0, k, g_all[:, 0, k:k + 1])
            x_add_last(0)
            dve.wait_ge(S("lb_exp"), 1)
            dve.tensor_tensor(lsum[:, :], e_logit[:, 0, :], e_logit[:, 1, :], ALU.add).then_inc(S("lb_step"), 1)
            dve.wait_ge(S("lb_step"), 3)
            dve.reciprocal(lsum[:, :], lsum[:, :]).then_inc(S("lb_step"), 1)
            dve.wait_ge(S("lb_step"), 4)
            dve.tensor_tensor(e_logit[:, :, :], e_logit[:, :, :], lsum[:, :].unsqueeze(1).broadcast_to([P, L, HG]),
                              ALU.mult).then_inc(S("lb_step"), 1)
            dve.wait_ge(S("lb_step"), 5)
            dve.tensor_tensor(cum[:, :, :], e_logit[:, :, :], e_logit[:, 0, :].unsqueeze(1).broadcast_to([P, L, HG]),
                              ALU.add).then_inc(S("lb_step"), 1)
            dve.wait_ge(S("lb_step"), 6)
            dve.tensor_tensor(g_all[:, 1, G_LB:G_OML], cum[:, 1, :], e_logit[:, 0, :], ALU.subtract)
            dve.tensor_tensor(g_all[:, 0, G_LB:G_OML], e_logit[:, 0, :], e_logit[:, 0, :], ALU.subtract)\
                .then_inc(S("lb_step"), 1)
            dve.wait_ge(S("lb_step"), 7)
            dve.tensor_scalar(g_all[:, 0:L, G_OML:G_END], g_all[:, 0:L, G_LB:G_OML], -1.0, 1.0, ALU.mult, ALU.add)
            for n in (1, 5):
                cols = slice(G_NORM + n * DK, G_NORM + (n + 1) * DK)
                dve.tensor_scalar(g_all[:, 0:L, cols], g_all[:, 0:L, cols], 0.5, None, ALU.mult)
            dve.memset(g_all[:, L, 0:DK], 1.0).then_inc(S("lb_step"), 1)
            dve.wait_ge(S("ident_loaded"), 16)
            dve.wait_ge(S("const_loaded"), 16 * 3)
            nc.vector.tensor_copy(mask[:, :, :], mask_raw[:, :, :]).then_inc(S("mask_ready"), 1)
            dve.wait_ge(S("mask_ready"), 1)
            with dve.Fori(0, L) as l:
                gate_up_phase(l, 0, GU_A)
                down_phase(l, 0, DOWN_A, SLOT)
                boundary(l, 0, g[:, G_NORM + 2 * DK:G_NORM + 3 * DK])
                mixer(l)
                gate_up_phase(l, 1, GU_B)
                down_phase(l, 1, DOWN_B, SLOT)
                boundary(l, 2, g_next)

        @block.gpsimd
        def _(pool):
            def norm_sum(before, k):
                pool.wait_ge(S("x_sq_ready"), before + (k + 1))
                if k == 1:
                    nc.gpsimd.tensor_tensor(x_acc[:, :], scr[:, 2, :], scr[:, 3, :], ALU.add)\
                        .then_inc(S("x_acc_ready"), 2)
                else:
                    pool.wait_ge(S("x_acc_ready"), before + k)
                    nc.gpsimd.tensor_tensor(x_acc[:, :], x_acc[:, :], scr[:, 2 + k % 6, :], ALU.add)\
                        .then_inc(S("x_acc_ready"), 1)

            def boundary(l, b):
                w_low(l, b)
                for k in range(1, DK - 1):
                    norm_sum(nth(l, 3 * DK, DK * (b + 1)), k)

            def w_low(l, b):
                n = (MIX, GU_B, SLOTS)[b] + 1
                for half in range(2):
                    cols = slice(half * SLOT // 2, (half + 1) * SLOT // 2)
                    if half == 0:
                        pool.wait_ge(S("hi_half"), nth(l, 3, b + 1))
                    else:
                        pool.wait_ge(S("split_done"), nth(l, SLOTS, n + 2))
                        pool.wait_ge(S("hi_ready"), nth(l, SLOTS, n + 1))
                    last = nc.gpsimd.tensor_tensor(w_lo[1][:, cols], raw[1][:, cols], w_hi[1][:, cols].bitcast(f32),
                                                   ALU.subtract)
                last.then_inc(S("split_done"), 1)

            def y_sum(l, b):
                base = b * DK
                pool.wait_ge(S("y_evac"), nth(l, 3 * DK, base + 4))
                nc.gpsimd.tensor_tensor(y_acc[:, :], scr[:, 0, :], scr[:, 1, :], ALU.add)\
                    .then_inc(S("y_acc_ready"), 2)
                for j in range(2, DK - 1):
                    pool.wait_ge(S("y_evac"), nth(l, 3 * DK, base + j + 3))
                    pool.wait_ge(S("y_acc_ready"), nth(l, 3 * DK, base + j + 2))
                    nc.gpsimd.tensor_tensor(y_acc[:, :], y_acc[:, :], scr[:, j % 2, :], ALU.add)\
                        .then_inc(S("y_acc_ready"), 1)

            def gate_up_phase(l, f):
                with pool.Fori(0, HALF) as i:
                    for e in range(2):
                        t = l * (2 * FT) + (i * 2 + (f * FT + e))
                        pool.wait_ge(S("gu_evac"), t + 3)
                        pool.wait_ge(S("a_lo_ready"), t + 1)
                        pool.wait_ge(S("sg_ready"), t + 3)
                        nc.gpsimd.tensor_tensor(scr[:, 6 + e, :], scr[:, 4 + e, :], scr[:, 2 + e, :], ALU.mult)\
                            .then_inc(S("a_ready"), 1)

            def keys_up(l, v):
                half = LEVELS[v - 1]
                n_tot = v - 3
                pool.wait_ge(S("level_done"), nth(l, NLEV, v))
                if n_tot:
                    pool.wait_ge(S("hk_up"), nth(l, NLEV - 2, n_tot))
                    pool.wait_ge(S("tot_up"), nth(l, NLEV - 2, n_tot))
                if half < 64:
                    k = hk[:, :, :].rearrange("p h (n two s) -> p (h n) two s", two=2, s=half)[:, :, 0, :]
                    second = tot[half][:, :, :].rearrange("p h (n two) -> p (h n) two", two=2)[:, :, 1]
                    second = second.unsqueeze(2).broadcast_to([P, second.shape[1], half])
                else:
                    k = hk[:, :, 0:TP].rearrange("p h (n two s) -> p h n two s", two=2, s=half)[:, :, :, 0, :]
                    second = tot[half][:, :, 0:4].rearrange("p h (n two) -> p h n two", two=2)[:, :, :, 1]
                    second = second.unsqueeze(3).broadcast_to([P, HG, 2, half])
                nc.gpsimd.tensor_tensor(k, k, second, ALU.mult).then_inc(S("hk_up"), 1)

            def mixer(l):
                pool.wait_ge(S("rstd_ready"), nth(l, 3, 2))
                pool.wait_ge(S("const_loaded"), 16 * 3)
                nc.gpsimd.tensor_tensor(scr[:, 0, :], cos[:, :], rstd[:, :], ALU.mult)
                nc.gpsimd.tensor_tensor(scr[:, 1, :], sin[:, :], rstd[:, :], ALU.mult).then_inc(S("cs_krr"), 1)
                pool.wait_ge(S("c_sq_ready"), nth(l, 5, 2))
                nc.gpsimd.tensor_tensor(c_acc[:, 0, :], c_sq[:, 0, :], c_sq[:, 1, :], ALU.add)\
                    .then_inc(S("c_acc_ready"), 2)
                pool.wait_ge(S("c_sq_ready"), nth(l, 5, 3))
                pool.wait_ge(S("c_acc_ready"), nth(l, 5, 2))
                nc.gpsimd.tensor_tensor(c_acc[:, 0, :], c_acc[:, 0, :], c_sq[:, 0, :], ALU.add)\
                    .then_inc(S("c_acc_ready"), 1)
                pool.wait_ge(S("c_sq_ready"), nth(l, 5, 5))
                nc.gpsimd.tensor_tensor(c_acc[:, 1, :], c_sq[:, 1, :], c_sq[:, 0, :], ALU.add)\
                    .then_inc(S("c_acc_ready"), 2)
                emptied(pool, l, ("m", M_KRS))
                nc.gpsimd.tensor_tensor(krr[:, :], kt1[:, :], kt2[:, :], ALU.add).then_inc(S("krr_ready"), 1)
                pool.wait_ge(S("cr_ready"), nth(l, 2, 1))
                nc.gpsimd.tensor_tensor(cos_r[:, :], cos[:, :], r_q[:, :], ALU.mult)
                nc.gpsimd.tensor_tensor(sin_r[:, :], sin[:, :], r_q[:, :], ALU.mult).then_inc(S("cs_q"), 1)
                wait_apart(pool, "job_done", nth(l, NJ, JOB["uq", 7] + 1))
                nc.gpsimd.memset(tri_p[:, :, :], 0.0)
                nc.gpsimd.memset(tri_s[:, :, :], 0.0).then_inc(S("tri_zero"), 1)
                for s in range(NG + 2):
                    if s - 2 in LAST_GROUP:
                        o_root(l, LAST_GROUP[s - 2])
                    v = s - FIRST_LEVEL_STEP
                    if 2 <= v < NLEV:
                        keys_up(l, v + 1)

            def o_root(l, qt):
                nq = QT[qt][1]
                pool.wait_ge(S("o_var_ready"), nth(l, 3, qt + 1))
                nc.gpsimd.tensor_tensor(rn[0:nq, qt:qt + 1], sv[0:nq, qt:qt + 1], minus_half[0:nq, 0:1], ALU.pow)\
                    .then_inc(S("o_rn_ready"), 1)

            nc.gpsimd.memset(minus_half[:, :], -0.5)
            nc.gpsimd.memset(row_ind[:, 64:P], 0.0)
            nc.gpsimd.memset(row_ind[:, 0:64], 1.0)
            nc.gpsimd.memset(neg[:, :], -1e30).then_inc(S("ones_ready"), 1)
            for k in range(1, DK - 1):
                norm_sum(0, k)
            pool.wait_ge(S("lb_step"), 8)
            with pool.Fori(0, L) as l:
                nc.gpsimd.tensor_copy(g[:, :], g_all[:, bass.ds(l, 1), :]).then_inc(S("gains_ready"), 1)
                gate_up_phase(l, 0)
                nc.gpsimd.tensor_copy(g_next[:, :], g_all[:, bass.ds(l + 1, 1), 0:DK]).then_inc(S("gains_ready"), 1)
                y_sum(l, 0)
                boundary(l, 0)
                mixer(l)
                y_sum(l, 1)
                boundary(l, 1)
                gate_up_phase(l, 1)
                y_sum(l, 2)
                boundary(l, 2)


def kernel(**inputs):
    import numpy as np
    import concourse.bacc as bacc
    from concourse.bass_utils import run_bass_kernel_spmd as run

    a = {n: np.asarray(v) for n, v in inputs.items()}

    def chunked(w, n):
        return w.reshape((L, n, P) + w.shape[2:]).swapaxes(1, 2)

    x = np.concatenate([a["x_prompt"][0], a["x_sample"][0]], axis=0)
    x_in = x.T.reshape(DK, P, T).transpose(1, 0, 2)
    per_layer = [a["norm_gains"].reshape(L, 6 * DK, P)] + [
        a[n].reshape(L, -1, P) for n in ("q_norm_gain", "kv_norm_gain", "mla_out_gain", "hg_norm_gain",
                                         "hg_lb_logits")]
    gains = np.concatenate(per_layer, axis=1).transpose(2, 0, 1)
    half = ROPE // 2
    inv = np.float32(10000.0) ** (-np.arange(half, dtype=np.float32) / np.float32(half))
    ang = (np.arange(T, dtype=np.float32)[:, None] * inv.astype(np.float32)).T
    cos_t = np.tile(np.cos(ang), (8, 1)).astype(np.float32)
    sin_t = np.tile(np.concatenate([-np.sin(ang), np.sin(ang)]), (4, 1)).astype(np.float32)
    mask = np.zeros((P, NLEV, 64), np.float32)
    q = np.arange(64)
    for v, hb in enumerate(LEVELS):
        t = 2 * q - hb if hb <= 0 else q // hb * 2 * hb + hb + q % hb
        key = np.arange(P)[:, None]
        mask[:, v, :] = key == t if hb <= 0 else key // hb == t // hb - 1

    def gate_up(w):
        return w.reshape(L, DK, P, 2, FT, P).transpose(0, 4, 2, 1, 3, 5).reshape(L, FT, P, SLOT)

    def down(w):
        return w.reshape(L, 2, HALF, P, DK, P).transpose(0, 4, 1, 3, 2, 5).reshape(L, 2 * DK, P, DOWN_W)

    def slots(w, rows, per_slot):
        n = w.shape[2] // (per_slot * P)
        w = w.reshape(L, rows, P, n, per_slot, P).transpose(0, 3, 2, 4, 1, 5).reshape(L, n, P, per_slot * rows * P)
        out = np.zeros((L, n, P, SLOT), w.dtype)
        out[..., :w.shape[3]] = w
        return out

    w_in = a["w_in"]
    c = CQ * P
    kr = w_in[:, :, c + CKV * P:c + CKV * P + ROPE]
    kr_swap = np.concatenate([kr[..., half:], kr[..., :half]], axis=-1)
    rest = w_in[:, :, c + CKV * P + ROPE:]
    n = HG * P
    hq, hf, rest = rest[..., :n], rest[..., n:2 * n], rest[..., 2 * n:]
    w_in = np.concatenate([w_in[:, :, :c + CKV * P]] + [kr] * 4 + [kr_swap] * 4 + [hf, hq, rest, rest[:, :, :P]],
                          axis=-1)
    s_in = slots(w_in, DK, 2)
    uq = a["w_uq"].reshape(L, CQ * P, H, QK)
    rope = uq[..., NOPE:]
    rope_swap = np.concatenate([rope[..., half:], rope[..., :half]], axis=-1)
    uq = np.concatenate([z.reshape(L, CQ * P, -1) for z in (uq[..., :NOPE], rope, rope_swap)], axis=-1)
    s_uq = slots(uq, CQ, 4)
    ukv = a["w_ukv"].reshape(L, CKV * P, H, NOPE + VD)
    s_kn = slots(ukv[..., :NOPE].reshape(L, CKV * P, H * NOPE), CKV, 4)
    v = ukv[..., NOPE:].reshape(L, 1, CKV, P, H * VD).transpose(0, 1, 3, 2, 4).reshape(L, 1, P, CKV * H * VD)
    s_v = np.zeros((L, 1, P, SLOT), v.dtype)
    s_v[..., :v.shape[3]] = v
    s_out = slots(a["w_out"], DK, 2)
    mix = np.concatenate([s_in[:, :6], s_uq, s_kn, s_v, s_in[:, 6:], s_out], axis=1)

    both = lambda x, y: np.stack([x, y], axis=1)
    given = {
        "x": x_in, "gains": gains, "cos": cos_t, "sin": sin_t, "ident": np.eye(P, dtype=np.float32), "mask": mask,
        "wgu": both(gate_up(a["ffa_w_gu"]), gate_up(a["ffb_w_gu"])).reshape(L * 2 * FT, P, SLOT),
        "wdn": both(down(a["ffa_w_down"]), down(a["ffb_w_down"])).reshape(L * 4 * DK, P, DOWN_W),
        "wmix": mix.reshape(L * MIX_SLOTS, P, SLOT),
        "latc": chunked(a["cache_mla_latent"][:, 0].swapaxes(1, 2), CKV),
        "krc": a["cache_mla_krope"][:, 0].swapaxes(1, 2),
        "s0": a["state_hgrn"][:, 0].transpose(0, 2, 1, 3),
    }
    nc = bacc.Bacc("TRN2", target_bir_lowering=False, num_devices=1)
    arrays, args = {}, []
    for name, arr in given.items():
        arr = np.ascontiguousarray(arr)
        arrays[f"in_{name}"] = arr
        args.append(nc.dram_tensor(f"in_{name}", arr.shape, mybir.dt.from_np(arr.dtype), kind="ExternalInput").ap())
    outs = {"x": (P, DK, T), "lat": (L, P, CKV, T), "kr": (L, ROPE, T), "st": (L, 2, P, HG, P)}
    for name, shape in outs.items():
        args.append(nc.dram_tensor(f"out_{name}", shape, mybir.dt.float32, kind="ExternalOutput").ap())
    trunk(nc, *args)
    r = run(nc, [arrays], core_ids=[0]).results[0]
    y = r["out_x"].transpose(2, 1, 0).reshape(T, D)
    lat = r["out_lat"].transpose(0, 3, 2, 1).reshape(L, T, CKV * P)
    kr = r["out_kr"].transpose(0, 2, 1)
    st = r["out_st"].transpose(0, 1, 3, 2, 4)
    return (y[None, :TP], y[None, TP:], lat[:, None, :TP], kr[:, None, :TP], st[:, 0][:, None],
            lat[:, None, TP:], kr[:, None, TP:], st[:, 1][:, None])
```
